# Optimizing a Trainium2 kernel written in Bass

```python
import math
import jax
import jax.numpy as jnp
from jax import lax
import numpy as np

D_MODEL = 1024
BATCH = 1
SEQ = 128
DEPTH = 2
DEC_BATCH = 1
DEC_SEQ = 256
PAST_LEN = 128

GRID_W = 64
BLOCK_Q = 128
ROPE_BASE = 10000.0
EPS = 1e-6
N_BRANCH = 4
BRANCH_WIDTH = D_MODEL // 2
A_HEAD_DIM = 64
A_HEADS = BRANCH_WIDTH // A_HEAD_DIM
A_KV_HEADS = 2
B_GROUPS = 4
B_GROUP_DIM = BRANCH_WIDTH // B_GROUPS
B_CHUNK = 128
C_HEADS = 4
C_HEAD_DIM = BRANCH_WIDTH // C_HEADS
C_CHUNK = 128
D_HEADS = 4
D_VDIM = BRANCH_WIDTH // D_HEADS
D_HALF_DIM = D_VDIM // 2
PEER_HEADS = 8
PEER_NKEYS = 128
PEER_EXPERTS = PEER_NKEYS * PEER_NKEYS
PEER_QDIM = 256
PEER_TOPK = 16
PEER_BLOCK = 128
ALPHA = (2 * DEPTH) ** 0.25
BETA = (8 * DEPTH) ** -0.25

IN_SPLITS = (A_HEADS * A_HEAD_DIM, A_KV_HEADS * A_HEAD_DIM, A_KV_HEADS * A_HEAD_DIM,
             BRANCH_WIDTH, BRANCH_WIDTH,
             BRANCH_WIDTH, BRANCH_WIDTH, BRANCH_WIDTH, BRANCH_WIDTH, 2 * 2 * C_HEADS,
             D_HEADS * 2 * D_HALF_DIM, D_HEADS * 2 * D_HALF_DIM, D_HEADS * D_VDIM,
             N_BRANCH * D_MODEL)
IN_WIDTH = sum(IN_SPLITS)
IN_SPLIT_POINTS = tuple(int(p) for p in np.cumsum(IN_SPLITS)[:-1])

kernel_name = 'hybrid_flow_backbone_step'

F32 = jnp.float32

def layer_norm(x, g, b):
    xf = x.astype(F32)
    mu = jnp.mean(xf, axis=-1, keepdims=True)
    var = jnp.mean(jnp.square(xf - mu), axis=-1, keepdims=True)
    return ((xf - mu) * lax.rsqrt(var + EPS) * g + b).astype(x.dtype)

def head_layer_norm(x, g):
    xf = x.astype(F32)
    mu = jnp.mean(xf, axis=-1, keepdims=True)
    var = jnp.mean(jnp.square(xf - mu), axis=-1, keepdims=True)
    return ((xf - mu) * lax.rsqrt(var + EPS) * g).astype(x.dtype)

def rms_norm(x, g):
    xf = x.astype(F32)
    return (xf * lax.rsqrt(jnp.mean(xf * xf, axis=-1, keepdims=True) + EPS) * g).astype(x.dtype)

def rope_2d(x):
    T, d = x.shape[1], x.shape[-1]
    rows = T // GRID_W
    row = jnp.repeat(jnp.arange(rows, dtype=F32), GRID_W)
    col = jnp.tile(jnp.arange(GRID_W, dtype=F32), rows)
    quarter = d // 4
    inv = ROPE_BASE ** (-jnp.arange(quarter, dtype=F32) / quarter)
    bshape = (T,) + (1,) * (x.ndim - 3) + (quarter,)
    xf = x.astype(F32)

    def rot(xa, pos):
        ang = (pos[:, None] * inv).reshape(bshape)
        cos, sin = jnp.cos(ang), jnp.sin(ang)
        x1, x2 = xa[..., :quarter], xa[..., quarter:]
        return jnp.concatenate([x1 * cos - x2 * sin, x2 * cos + x1 * sin], axis=-1)

    return jnp.concatenate([rot(xf[..., :2 * quarter], row), rot(xf[..., 2 * quarter:], col)], axis=-1).astype(x.dtype)

def gqa_attend(q, k, v):
    B, T, H, d = q.shape
    G = k.shape[2]
    R = H // G
    nb = T // BLOCK_Q
    qb = q.reshape(B, nb, BLOCK_Q, G, R, d).transpose(1, 0, 2, 3, 4, 5)
    scale = d ** -0.5

    def one(qblk):
        s = jnp.einsum('bqgrd,bkgd->bgrqk', qblk, k).astype(F32) * scale
        p = jax.nn.softmax(s, axis=-1).astype(v.dtype)
        return jnp.einsum('bgrqk,bkgd->bqgrd', p, v)

    o = lax.map(one, qb)
    return o.transpose(1, 0, 2, 3, 4, 5).reshape(B, T, H * d)

def diff_attend(q, k, v, lam):
    B, T, H, _, d = q.shape
    nb = T // BLOCK_Q
    qb = q.reshape(B, nb, BLOCK_Q, H, 2, d).transpose(1, 0, 2, 3, 4, 5)
    scale = d ** -0.5

    def one(qblk):
        s = jnp.einsum('bqhjd,bkhjd->bhjqk', qblk, k).astype(F32) * scale
        p = jax.nn.softmax(s, axis=-1)
        a = (p[:, :, 0] - lam * p[:, :, 1]).astype(v.dtype)
        return jnp.einsum('bhqk,bkhe->bqhe', a, v)

    o = lax.map(one, qb)
    return o.transpose(1, 0, 2, 3, 4).reshape(B, T, H, v.shape[-1])

def chunk_mlp(u, v, ws, bias):
    B, T, _ = v.shape
    nc = T // B_CHUNK
    vf = v.astype(F32)
    mu = jnp.mean(vf, axis=-1, keepdims=True)
    var = jnp.mean(jnp.square(vf - mu), axis=-1, keepdims=True)
    vn = ((vf - mu) * lax.rsqrt(var + EPS)).astype(v.dtype).reshape(B, nc, B_CHUNK, B_GROUPS, B_GROUP_DIM)
    s = jnp.einsum('gpq,bcqgd->bcpgd', ws, vn) + bias.T[None, None, :, :, None]
    return u * s.reshape(B, T, BRANCH_WIDTH)

def mlstm_chunkwise(q, k, v, ig, lf, C0, n0, m0):
    B, T, H, d = q.shape
    nc = T // C_CHUNK
    L = C_CHUNK

    def to_chunks(a):
        return a.reshape(B, nc, L, H, d).transpose(1, 0, 3, 2, 4)

    def gates_to_chunks(a):
        return a.reshape(B, nc, L, H).transpose(1, 0, 3, 2)

    causal = jnp.tril(jnp.ones((L, L), dtype=bool))

    def step(carry, xs):
        C, n, m = carry
        qc, kc, vc, ic, fc = xs
        qf, kf, vf = qc.astype(F32), kc.astype(F32), vc.astype(F32)
        b = jnp.cumsum(fc, axis=-1)
        dlog = jnp.where(causal, b[..., :, None] - b[..., None, :] + ic[..., None, :], -jnp.inf)
        m_t = jnp.maximum(jnp.max(dlog, axis=-1), b + m[..., None])
        w = jnp.einsum('bhtd,bhsd->bhts', qf, kf) * jnp.exp(dlog - m_t[..., None])
        inter = jnp.exp(b + m[..., None] - m_t)
        num = jnp.einsum('bhts,bhsd->bhtd', w, vf) + inter[..., None] * jnp.einsum('bhtd,bhde->bhte', qf, C)
        den = jnp.sum(w, axis=-1) + inter * jnp.einsum('bhtd,bhd->bht', qf, n)
        h = num / jnp.maximum(jnp.abs(den), jnp.exp(-m_t))[..., None]
        b_last = b[..., -1]
        g = b_last[..., None] - b + ic
        m_new = jnp.maximum(b_last + m, jnp.max(g, axis=-1))
        decay = jnp.exp(b_last + m - m_new)
        ws = jnp.exp(g - m_new[..., None])
        C_new = decay[..., None, None] * C + jnp.einsum('bhs,bhsd,bhse->bhde', ws, kf, vf)
        n_new = decay[..., None] * n + jnp.einsum('bhs,bhsd->bhd', ws, kf)
        return (C_new, n_new, m_new), h.astype(q.dtype)

    init = (C0.astype(F32), n0.astype(F32), m0.astype(F32))
    xs = (to_chunks(q), to_chunks(k), to_chunks(v), gates_to_chunks(ig), gates_to_chunks(lf))
    (C, n, m), hs = lax.scan(step, init, xs)
    h = hs.transpose(1, 0, 3, 2, 4).reshape(B, T, H, d)
    return h, C, n, m

def mlstm_branch(q, k, v, o, graw, gate_bias, gn, init):
    B, T = q.shape[:2]
    k = k * (C_HEAD_DIM ** -0.5)
    gts = graw.reshape(B, T, 2, 2, C_HEADS).astype(F32) + gate_bias.astype(F32)
    if init is None:
        C0 = jnp.zeros((B, 2, C_HEADS, C_HEAD_DIM, C_HEAD_DIM), F32)
        n0 = jnp.zeros((B, 2, C_HEADS, C_HEAD_DIM), F32)
        m0 = jnp.zeros((B, 2, C_HEADS), F32)
    else:
        C0, n0, m0 = init
    h_f, C_f, n_f, m_f = mlstm_chunkwise(q, k, v, gts[:, :, 0, 0], jax.nn.log_sigmoid(gts[:, :, 0, 1]),
                                         C0[:, 0], n0[:, 0], m0[:, 0])
    fl = lambda a: jnp.flip(a, axis=1)
    h_b, C_b, n_b, m_b = mlstm_chunkwise(fl(q), fl(k), fl(v), fl(gts[:, :, 1, 0]),
                                         fl(jax.nn.log_sigmoid(gts[:, :, 1, 1])),
                                         C0[:, 1], n0[:, 1], m0[:, 1])
    h = h_f + fl(h_b)
    y = head_layer_norm(h, gn).reshape(B, T, BRANCH_WIDTH) * jax.nn.sigmoid(o)
    state = (jnp.stack([C_f, C_b], axis=1), jnp.stack([n_f, n_b], axis=1), jnp.stack([m_f, m_b], axis=1))
    return y, state

def merge_branches(ys, gates, w_branch, w_out):
    B, T, _ = gates.shape
    g = jax.nn.sigmoid(gates.reshape(B, T, N_BRANCH, D_MODEL))
    proj = jnp.einsum('btne,ned->btnd', jnp.stack(ys, axis=2), w_branch)
    return jnp.sum(g * proj, axis=2) @ w_out

def peer_ffn(h, wq, keys, u, v):
    B, T, D = h.shape
    N = B * T
    x = h.reshape(N, D)
    q = (x @ wq).reshape(N, PEER_HEADS, 2, PEER_QDIM // 2)
    s = jnp.einsum('nhpd,hpkd->nhpk', q, keys).astype(F32)
    s1, i1 = lax.top_k(s[:, :, 0], PEER_TOPK)
    s2, i2 = lax.top_k(s[:, :, 1], PEER_TOPK)
    cand = (s1[..., :, None] + s2[..., None, :]).reshape(N, PEER_HEADS, PEER_TOPK * PEER_TOPK)
    best, pos = lax.top_k(cand, PEER_TOPK)
    e1 = jnp.take_along_axis(i1, pos // PEER_TOPK, axis=-1)
    e2 = jnp.take_along_axis(i2, pos % PEER_TOPK, axis=-1)
    experts = (e1 * PEER_NKEYS + e2).reshape(N, PEER_HEADS * PEER_TOPK)
    gate = jax.nn.softmax(best, axis=-1).reshape(N, PEER_HEADS * PEER_TOPK).astype(h.dtype)
    nb = N // PEER_BLOCK

    def one(args):
        xb, eb, gb = args
        a = jax.nn.gelu(jnp.einsum('nkd,nd->nk', u[eb], xb), approximate=False)
        return jnp.einsum('nk,nkd->nd', gb * a, v[eb])

    out = lax.map(one, (x.reshape(nb, PEER_BLOCK, D), experts.reshape(nb, PEER_BLOCK, -1),
                        gate.reshape(nb, PEER_BLOCK, -1)))
    return out.reshape(B, T, D)

def trunk_layer(x, mod, lp, layer_idx, ctx):
    B, T, _ = x.shape
    sh1, sc1, g1, sh2, sc2, g2 = jnp.split(mod, 6, axis=-1)
    h = x * (1.0 + sc1) + sh1
    (aq, ak, av, bu, bv, cq, ck, cv, co, cg, dq, dk, dv, gates) = jnp.split(h @ lp['w_in'], IN_SPLIT_POINTS, axis=-1)
    aq = rms_norm(aq.reshape(B, T, A_HEADS, A_HEAD_DIM), lp['attn_qk_gain'][0])
    ak = rms_norm(ak.reshape(B, T, A_KV_HEADS, A_HEAD_DIM), lp['attn_qk_gain'][1])
    av = av.reshape(B, T, A_KV_HEADS, A_HEAD_DIM)
    cq = cq.reshape(B, T, C_HEADS, C_HEAD_DIM)
    ck = ck.reshape(B, T, C_HEADS, C_HEAD_DIM)
    cv = cv.reshape(B, T, C_HEADS, C_HEAD_DIM)
    dq = dq.reshape(B, T, D_HEADS, 2, D_HALF_DIM)
    dk = dk.reshape(B, T, D_HEADS, 2, D_HALF_DIM)
    dv = dv.reshape(B, T, D_HEADS, D_VDIM)
    lam_init = 0.8 - 0.6 * math.exp(-0.3 * layer_idx)
    lv = lp['diff_lambda'].astype(F32)
    lam = jnp.exp(jnp.sum(lv[0] * lv[1])) - jnp.exp(jnp.sum(lv[2] * lv[3])) + lam_init
    if ctx is None:
        ya = gqa_attend(aq, ak, av)
        yd = diff_attend(dq, dk, dv, lam)
        yc, c_state = mlstm_branch(cq, ck, cv, co, cg, lp['mlstm_gate_bias'], lp['mlstm_gn'], None)
        new_state = (ak, av, dk, dv, c_state[0], c_state[1], c_state[2])
    else:
        cak, cav, cdk, cdv, cC, cn, cm = ctx
        ya = gqa_attend(rope_2d(aq),
                        jnp.concatenate([rope_2d(ak), cak.astype(ak.dtype)], axis=1),
                        jnp.concatenate([av, cav.astype(av.dtype)], axis=1))
        yd = diff_attend(rope_2d(dq),
                         jnp.concatenate([rope_2d(dk), cdk.astype(dk.dtype)], axis=1),
                         jnp.concatenate([dv, cdv.astype(dv.dtype)], axis=1), lam)
        yc, _ = mlstm_branch(cq, ck, cv, co, cg, lp['mlstm_gate_bias'], lp['mlstm_gn'], (cC, cn, cm))
        new_state = None
    yb = chunk_mlp(bu, bv, lp['gmlp_ws'], lp['gmlp_b'])
    yd = (rms_norm(yd, lp['diff_gn']) * (1.0 - lam_init)).reshape(B, T, BRANCH_WIDTH)
    y = merge_branches((ya, yb, yc, yd), gates, lp['w_branch'], lp['w_out'])
    x = layer_norm(ALPHA * x + g1 * y, lp['ln_g'][0], lp['ln_b'][0])
    h2 = x * (1.0 + sc2) + sh2
    f = peer_ffn(h2, lp['peer_wq'], lp['peer_keys'], lp['peer_u'], lp['peer_v'])
    x = layer_norm(ALPHA * x + g2 * f, lp['ln_g'][1], lp['ln_b'][1])
    return x, new_state

def setup_inputs(seed: int = 0) -> dict:
    key = jax.random.key(seed)
    ks = jax.random.split(key, 32)

    def nrm(k, shape, s):
        return jax.random.normal(k, shape, F32) * s

    D = D_MODEL
    return {
        'x_prompt': nrm(ks[0], (BATCH, SEQ, D), 1.0),
        'x_sample': nrm(ks[1], (DEC_BATCH, DEC_SEQ, D), 1.0),
        'cache_a_k': nrm(ks[2], (DEC_BATCH, DEPTH, PAST_LEN, A_KV_HEADS, A_HEAD_DIM), 1.0),
        'cache_a_v': nrm(ks[3], (DEC_BATCH, DEPTH, PAST_LEN, A_KV_HEADS, A_HEAD_DIM), 1.0),
        'cache_d_k': nrm(ks[4], (DEC_BATCH, DEPTH, PAST_LEN, D_HEADS, 2, D_HALF_DIM), 1.0),
        'cache_d_v': nrm(ks[5], (DEC_BATCH, DEPTH, PAST_LEN, D_HEADS, D_VDIM), 1.0),
        'state_c_C': nrm(ks[6], (DEC_BATCH, DEPTH, 2, C_HEADS, C_HEAD_DIM, C_HEAD_DIM), 0.05),
        'state_c_n': nrm(ks[7], (DEC_BATCH, DEPTH, 2, C_HEADS, C_HEAD_DIM), 0.5),
        'state_c_m': nrm(ks[8], (DEC_BATCH, DEPTH, 2, C_HEADS), 0.5),
        'c': nrm(ks[9], (DEC_BATCH, D), 1.0),
        'c_ctx': nrm(ks[10], (D,), 1.0),
        'w_mod': nrm(ks[11], (DEPTH, D, 6 * D), 0.5 * D ** -0.5),
        'b_mod': nrm(ks[12], (DEPTH, 6 * D), 0.02),
        'w_in': nrm(ks[13], (DEPTH, D, IN_WIDTH), D ** -0.5),
        'attn_qk_gain': 1.0 + nrm(ks[14], (DEPTH, 2, A_HEAD_DIM), 0.02),
        'gmlp_ws': nrm(ks[15], (DEPTH, B_GROUPS, B_CHUNK, B_CHUNK), B_CHUNK ** -0.5),
        'gmlp_b': 1.0 + nrm(ks[16], (DEPTH, B_GROUPS, B_CHUNK), 0.02),
        'mlstm_gate_bias': nrm(ks[17], (DEPTH, 2, 2, C_HEADS), 0.1) + jnp.array([0.0, 3.0], F32)[None, None, :, None],
        'mlstm_gn': 1.0 + nrm(ks[18], (DEPTH, C_HEADS, C_HEAD_DIM), 0.02),
        'diff_lambda': nrm(ks[19], (DEPTH, 4, D_HALF_DIM), 0.1),
        'diff_gn': 1.0 + nrm(ks[20], (DEPTH, D_HEADS, D_VDIM), 0.02),
        'w_branch': nrm(ks[21], (DEPTH, N_BRANCH, BRANCH_WIDTH, D), BRANCH_WIDTH ** -0.5),
        'w_out': nrm(ks[22], (DEPTH, D, D), BETA * D ** -0.5),
        'ln_g': 1.0 + nrm(ks[23], (DEPTH, 2, D), 0.02),
        'ln_b': nrm(ks[24], (DEPTH, 2, D), 0.02),
        'peer_wq': nrm(ks[25], (DEPTH, D, PEER_HEADS * PEER_QDIM), D ** -0.5),
        'peer_keys': nrm(ks[26], (DEPTH, PEER_HEADS, 2, PEER_NKEYS, PEER_QDIM // 2), (PEER_QDIM // 2) ** -0.5),
        'peer_u': nrm(ks[27], (DEPTH, PEER_EXPERTS, D), D ** -0.5),
        'peer_v': nrm(ks[28], (DEPTH, PEER_EXPERTS, D), BETA),
    }

def reference(x_prompt, x_sample, cache_a_k, cache_a_v, cache_d_k, cache_d_v, state_c_C, state_c_n, state_c_m,
              c, c_ctx, w_mod, b_mod, w_in, attn_qk_gain, gmlp_ws, gmlp_b, mlstm_gate_bias, mlstm_gn,
              diff_lambda, diff_gn, w_branch, w_out, ln_g, ln_b, peer_wq, peer_keys, peer_u, peer_v):
    y_p = x_prompt
    y_s = x_sample
    st_ak, st_av, st_dk, st_dv, st_C, st_n, st_m = [], [], [], [], [], [], []
    for l in range(DEPTH):
        lp = {'w_in': w_in[l], 'attn_qk_gain': attn_qk_gain[l], 'gmlp_ws': gmlp_ws[l], 'gmlp_b': gmlp_b[l],
              'mlstm_gate_bias': mlstm_gate_bias[l], 'mlstm_gn': mlstm_gn[l], 'diff_lambda': diff_lambda[l],
              'diff_gn': diff_gn[l], 'w_branch': w_branch[l], 'w_out': w_out[l], 'ln_g': ln_g[l], 'ln_b': ln_b[l],
              'peer_wq': peer_wq[l], 'peer_keys': peer_keys[l], 'peer_u': peer_u[l], 'peer_v': peer_v[l]}
        mod_ctx = (jax.nn.silu(c_ctx) @ w_mod[l] + b_mod[l])[None, None, :]
        y_p, st = trunk_layer(y_p, mod_ctx, lp, l, None)
        st_ak.append(st[0]); st_av.append(st[1]); st_dk.append(st[2]); st_dv.append(st[3])
        st_C.append(st[4]); st_n.append(st[5]); st_m.append(st[6])
        mod_lat = (jax.nn.silu(c) @ w_mod[l] + b_mod[l])[:, None, :]
        ctx = (cache_a_k[:, l], cache_a_v[:, l], cache_d_k[:, l], cache_d_v[:, l],
               state_c_C[:, l], state_c_n[:, l], state_c_m[:, l])
        y_s, _ = trunk_layer(y_s, mod_lat, lp, l, ctx)
    new_a_k = jnp.stack(st_ak, axis=1)
    new_a_v = jnp.stack(st_av, axis=1)
    new_d_k = jnp.stack(st_dk, axis=1)
    new_d_v = jnp.stack(st_dv, axis=1)
    new_c_C = jnp.stack(st_C, axis=1)
    new_c_n = jnp.stack(st_n, axis=1)
    new_c_m = jnp.stack(st_m, axis=1)
    return (y_p, y_s, new_a_k, new_a_v, new_d_k, new_d_v, new_c_C, new_c_n, new_c_m)


_drawn_inputs = setup_inputs


def setup_inputs(seed=0):
    import zlib

    import numpy as np

    out = dict(_drawn_inputs(seed))
    spreads = {}
    factors = {'cache_a_k': 8.0,
     'cache_a_v': 8.0,
     'cache_d_k': 3.332,
     'cache_d_v': 2.949,
     'state_c_C': 8.0,
     'state_c_n': 8.0,
     'state_c_m': 8.0,
     'attn_qk_gain': 2.736,
     'gmlp_b': 22.829,
     'mlstm_gn': 35.915,
     'diff_lambda': 8.0,
     'diff_gn': 28.988}
    for name, (base, spread) in spreads.items():
        noise = np.random.default_rng([zlib.crc32(name.encode()), seed]).standard_normal(out[name].shape)
        drawn = base * np.exp(spread * noise) if base else spread * noise
        out[name] = jnp.asarray(drawn.astype(out[name].dtype))
    for name, factor in factors.items():
        out[name] = (out[name] * factor).astype(out[name].dtype)
    return out
```

```python
import math
from contextlib import ExitStack

import concourse.bass as bass
from concourse import mybir

DM = 1024
DEPTH = 2
P = 128
TILES = 3
T = TILES * P
KC = DM // P
BW = DM // 2
AH, AG, AD = 8, 2, 64
CH, CD = 4, 128
DH, DD, DV = 4, 64, 128
BG = 4
NB = 4
GW = 64
PH, PKEYS, PTOP, PQ = 8, 128, 16, 128
EXPERTS = PKEYS * PKEYS
PICKS = PH * PTOP
EPS = 1e-6
ALPHA = (2 * DEPTH) ** 0.25
NEG = -1.0e30

C_AQ, C_AK, C_BU, C_BV, C_CQ, C_CK, C_CV, C_CO, C_CG, C_DQ, C_DK, C_DVV = (
    0, 512, 768, 1280, 1792, 2304, 2816, 3328, 3840, 3856, 4368, 4880)
C_GATES = 5392
BLOCKS = [("aq", C_AQ, 512), ("akv", C_AK, 256), ("dq", C_DQ, 512), ("dk", C_DK, 512),
          ("dv", C_DVV, 512), ("cg", C_CG, 16), ("cq", C_CQ, 512), ("ck", C_CK, 512),
          ("cv", C_CV, 512), ("bv", C_BV, 512), ("bu", C_BU, 512), ("co", C_CO, 512)]
BLK = {name: i for i, (name, _, _) in enumerate(BLOCKS)}

KEY_SLOT_OF_TILE = {1: 0, 2: 1, 3: 2, 0: 3}
TILE_OF_KEY_SLOT = [1, 2, 3, 0]
KEY_SLOTS = {0: [3], 1: [0, 1, 2], 2: [0, 1, 2]}

C_UNITS = [(0, 0), (0, 1), (1, 0), (2, 1), (2, 0), (1, 1)]
C_FIRST = {0: 0, 1: 2, 2: 3}
C_UPDATES = (0, 1, 2, 3)

A_UNITS = [(t, h) for t in range(TILES) for h in range(AH)]
D_UNITS = [(t, h) for t in range(TILES) for h in range(DH)]
LAG_T, LAG_V = 2, 3

FIRST_BLOCKS = 4
_REST = [(b, t) for b in range(FIRST_BLOCKS, len(BLOCKS)) for t in range(TILES)]
A_FILL = {2 * k: _REST[k] for k in range(14)}
D_FILL = {2 * k + 1: _REST[14 + k] for k in range(7)}
LAST_FILL = _REST[21:]

MERGE_ORDER = (0, 3, 1, 2)
MERGES = [(n, j) for n in MERGE_ORDER for j in range(KC)]
GAP = 2
C_FILL = [MERGES[GAP * g:GAP * (g + 1)] for g in range(2 * len(C_UNITS))]
LAST_MERGES = MERGES[GAP * 2 * len(C_UNITS):]
assert [n for n, _ in LAST_MERGES] == [2] * KC

SLOTS = 8
ROUNDS = PICKS // SLOTS


def mod_jobs(l):
    out = []
    for j in range(12):
        out.append(("mod", l, j))
        if j // 2 in (0, 1, 3, 4):
            out.append(("mcol", l, j))
    return out


def tensor_jobs():
    out = mod_jobs(0)
    for l in range(DEPTH):
        out += [("xT", l, t, hf) for t in range(TILES) for hf in range(2)]
        out += [("proj", l, b, t) for b in range(FIRST_BLOCKS) for t in range(TILES)]
        out += [("wsT", l)]
        out += [("qTA", l, t) for t in range(TILES)] + [("kTA", l, s) for s in range(4)]
        for i in range(len(A_UNITS) + LAG_V):
            if i < len(A_UNITS):
                out.append(("sA", l, i))
            if 0 <= i - LAG_T < len(A_UNITS):
                out.append(("pTA", l, i - LAG_T))
            if i >= LAG_V and (i - LAG_V) % AH == 0:
                out.append(("oA", l, (i - LAG_V) // AH))
            if i in A_FILL:
                out.append(("proj", l, *A_FILL[i]))
        out += [("qTD", l, t) for t in range(TILES)] + [("kTD", l, s) for s in range(4)]
        for i in range(len(D_UNITS) + LAG_V):
            if i < len(D_UNITS):
                out += [("sD", l, i, 0), ("sD", l, i, 1)]
            if 0 <= i - LAG_T < len(D_UNITS):
                out.append(("pTD", l, i - LAG_T))
            if i >= LAG_V and (i - LAG_V) % DH == 0:
                out.append(("oD", l, (i - LAG_V) // DH))
            if i in D_FILL:
                out.append(("proj", l, *D_FILL[i]))
        out += [("proj", l, b, t) for b, t in LAST_FILL]
        out += [("bmm", l, t) for t in range(TILES)]
        out += [("qTC", l, t) for t in range(TILES)] + [("kTC", l, t) for t in range(TILES)]
        out += [("sC", l, t) for t in range(TILES)]
        out += [("yT", l, n, t) for n in (0, 1) for t in range(TILES)]
        out += [("cum", l)]
        out += [("yT", l, 3, t) for t in range(TILES)]
        for u, (t, d) in enumerate(C_UNITS):
            out += [("rb", l, u)]
            for n, j in C_FILL[2 * u]:
                out += [("gate", l, n, j), ("br", l, n, j)]
            out += [("wT", l, u)]
            if u in C_UPDATES:
                out += [("kv", l, u, 0), ("kv", l, u, 1)]
            out += [("num", l, u, 0), ("num", l, u, 1)]
            if t:
                out += [("qC", l, u, 0), ("qC", l, u, 1)]
            for n, j in C_FILL[2 * u + 1]:
                out += [("gate", l, n, j), ("br", l, n, j)]
        out += [("yT", l, 2, t) for t in range(TILES)]
        for n, j in LAST_MERGES:
            out += [("gate", l, n, j), ("br", l, n, j)]
        out += [("out", l, hf, t) for hf in range(2) for t in range(TILES)]
        for t in range(TILES):
            out += [("x2T", l, t, 0), ("x2T", l, t, 1)]
        for t in range(TILES):
            out += [("h2", l, t, 0), ("h2", l, t, 1)]
        out += [("q", l, j) for j in range(2 * PH)]
        out += [("kT", l, i) for i in range(4)]
        out += [("sc", l, t, i) for t in range(TILES) for i in range(4)]
        if l + 1 < DEPTH:
            out += mod_jobs(l + 1)
    return out


HELD = {"oA": (6, 7), "oD": (6, 7)}
BANKS = 6


def turns(jobs):
    used, out, i, held = [0] * 8, {}, 0, 0
    for j in jobs:
        if j[0] in HELD:
            b = HELD[j[0]][held % 2]
            held += 1
        else:
            b = i % BANKS
            i += 1
        out[j] = (b, used[b])
        used[b] += 1
    return out


N_PARAMS = 16
RING = 3
SLOT_W = KC * 512


def weight_loads():
    out = [(("mod", 0, j), ("mod", 0, j)) for j in range(12)]
    for l in range(DEPTH):
        out += [(("proj", l, b), ("proj", l, b, TILES - 1)) for b in range(len(BLOCKS))]
        for n in MERGE_ORDER:
            out += [(("wg", l, n, 0), ("gate", l, n, 3)), (("wb", l, n), ("br", l, n, 7)),
                    (("wg", l, n, 1), ("gate", l, n, 7))]
        out += [(("out", l, hf), ("out", l, hf, TILES - 1)) for hf in range(2)]
        out += [(("q", l, c), ("q", l, 4 * c + 3)) for c in range(4)]
        out += [(("keys", l), ("kT", l, 3))]
        if l + 1 < DEPTH:
            out += [(("mod", l + 1, j), ("mod", l + 1, j)) for j in range(12)]
    return out


def build(nc, x_prompt, x_sample, cache_a_k, cache_a_v, cache_d_k, cache_d_v, state_c_C, state_c_n,
          state_c_m, c, c_ctx, w_mod, b_mod, w_in, attn_qk_gain, gmlp_ws, gmlp_b, mlstm_gate_bias,
          mlstm_gn, diff_lambda, diff_gn, w_branch, w_out, ln_g, ln_b, peer_wq, peer_keys, peer_u,
          peer_v, consts, y_prompt, y_sample, new_a_k, new_a_v, new_d_k, new_d_v, new_c_C, new_c_n,
          new_c_m):
    f32, u32 = mybir.dt.float32, mybir.dt.uint32
    ALU, ACT, X = mybir.AluOpType, mybir.ActivationFunctionType, mybir.AxisListType.X
    ctx = ExitStack()
    with ctx:
        def sb(name, width, dt=f32, parts=P):
            return ctx.enter_context(nc.sbuf_tensor(name, [parts, width], dt))[:, :]

        named = {}

        def sem(name):
            if name not in named:
                named[name] = ctx.enter_context(nc.semaphore(name))
            return named[name]

        x = sb("x", TILES * DM).rearrange("p (t d) -> p t d", t=TILES)
        hT = sb("hT", KC * T).rearrange("p (c t) -> p c t", c=KC)
        ring = sb("ring", RING * SLOT_W).rearrange("p (s n) -> p s n", s=RING)
        work = sb("work", 3076)
        cst = sb("cst", 1024 + 32)
        pars = sb("pars", 1180)
        states = sb("states", 2 * 2 * CH * (CD + 1))
        small = sb("small", 512)
        ARENA = 26684
        arena = sb("arena", ARENA)
        top = [0]

        def take(width):
            at = top[0]
            top[0] += width
            assert top[0] <= ARENA, top[0]
            return arena[:, at:at + width]

        def tiled(width, n=TILES):
            return take(width * n).rearrange("p (t d) -> p t d", t=n)

        aq, akv, bu, bv = tiled(512), tiled(256, 4), tiled(512), tiled(512)
        c_at = top[0]
        cq, ck = tiled(512), tiled(512)
        cv = tiled(CH * (CD + 1)).rearrange("p t (h e) -> p t h e", h=CH)
        co, cg, dq = tiled(512), tiled(16), tiled(512)
        d_at = top[0]
        dk, dv = tiled(512, 4), tiled(512, 4)
        qTA, kTA = take(4 * T).rearrange("p (b t) -> p b t", b=4), take(2 * 512).rearrange("p (g k) -> p g k", g=2)
        qTD, kTD = take(4 * T).rearrange("p (b t) -> p b t", b=4), take(4 * 512).rearrange("p (g k) -> p g k", g=4)
        q_at = top[0]
        qTC, kTC = take(4 * T).rearrange("p (b t) -> p b t", b=4), take(4 * T).rearrange("p (b t) -> p b t", b=4)
        wsT = arena[:, q_at + 512:q_at + 1024].rearrange("p (g q) -> p g q", g=BG)
        ws_raw = arena[:, q_at:q_at + 512].rearrange("p (g q) -> p g q", g=BG)
        k_dup = arena[:, q_at + 4 * T:q_at + 4 * T + 1024].rearrange("p (s g n) -> p s g n", s=4, g=AG)
        sC = cq
        merged = arena[:, d_at:d_at + KC * T].rearrange("p (c t) -> p c t", c=KC)
        yA, yB, yC, yD = aq, bv, dq, dk[:, 0:TILES, :]
        ys = [yA, yB, yC, yD]
        yT = [qTA, bu.rearrange("p t d -> p (t d)").rearrange("p (b t) -> p b t", b=4), qTC, qTD]
        gl1 = arena[:, c_at:c_at + 4 * DM].rearrange("p (a d) -> p a d", a=4)
        top[0] = 0
        h2 = tiled(DM)
        qTp = take(16 * T).rearrange("p (b t) -> p b t", b=16)
        keysT = take(16 * P).rearrange("p (b k) -> p b k", b=16)
        S = take(16 * PKEYS).rearrange("p (b k) -> p b k", b=16)
        cand = take(2048)
        rep = take(2048)
        rows = take(SLOTS * DM).rearrange("p (s d) -> p s d", s=SLOTS)
        acc = take(DM)
        gl2 = hT.rearrange("p c t -> p (c t)").rearrange("p (a d) -> p a d", a=3)

        pr = work[:, 0:6 * 384].rearrange("p (s k) -> p s k", s=6)
        pt = work[:, 6 * 384:8 * 384].rearrange("p (s k) -> p s k", s=2)
        diag = work[:, 0:512].rearrange("p (h s) -> p h s", h=CH)
        kws = diag
        Mx = work[:, 512:1024].rearrange("p (h s) -> p h s", h=CH)
        Wc = work[:, 1024:1536].rearrange("p (h s) -> p h s", h=CH)
        WT = work[:, 1536:2048].rearrange("p (h s) -> p h s", h=CH)
        ND = work[:, 2048:2048 + CH * (CD + 1)].rearrange("p (h e) -> p h e", h=CH)
        tmp = work[:, 2564:2564 + 512]
        kd_flat = kTD.rearrange("p g k -> p (g k)")
        sg = kd_flat[:, 0:2 * T].rearrange("p (s k) -> p s k", s=2)
        prod = kd_flat[:, 2 * T:3 * T]
        z = work[:, 0:512]
        m_stage = work[0:2, 0:1024].rearrange("p (s n) -> p s n", s=2)
        b_stage = work[0:2, 1024:2048].rearrange("p (s n) -> p s n", s=2)

        ident, ones = cst[:, 0:128], cst[:, 128:256]
        tri = cst[:, 256:512].rearrange("p (a t) -> p a t", a=2)
        negmask = cst[:, 512:768].rearrange("p (a t) -> p a t", a=2)
        rope_cs = cst[:, 768:1024].rearrange("p (a t d) -> p a t d", a=2, t=2)
        iota16 = cst[:, 1024:1040]
        nhalf = cst[:, 1040:1056]

        gains = pars[:, 0:128].rearrange("p (a d) -> p a d", a=2)
        cg_bias = pars[:, 128:144]
        b_bias = pars[:, 144:148]
        lam_v = kTD[:, 0, 0:256].rearrange("p (a b d) -> p a b d", a=2, b=2)
        gn = pars[:, 148:660]
        dgn = pars[:, 660:1172]
        neg_lam = pars[:, 1172:1173]
        lam_e = pars[:, 1174:1176]

        SW = CH * (CD + 1)
        c_state = states[:, 0:2 * SW].rearrange("p (a h e) -> p a h e", a=2, h=CH)
        c_new = states[:, 2 * SW:4 * SW].rearrange("p (a h e) -> p a h e", a=2, h=CH)

        modcol = small[:, 0:128].rearrange("p (l a c n) -> p l a c n", l=DEPTH, a=4, c=KC)
        silu_c = small[:, 128:144].rearrange("p (c n) -> p c n", c=KC)
        sig_c = small[:, 144:160].rearrange("p (c n) -> p c n", c=KC)
        negm = small[:, 160:184]
        sums = small[:, 184:208]
        rsum = small[:, 208:232]
        ms = small[:, 232:248]
        rs = small[:, 248:264]
        stats = small[:, 264:264 + 24].rearrange("p (a s) -> p a s", a=4)
        aggr = small[:, 288:296].rearrange("p (a s) -> p a s", a=4)
        m_lat = small[:, 296:304].rearrange("p (a h) -> p a h", a=2)
        m_out = small[:, 304:312].rearrange("p (a h) -> p a h", a=2)
        lf = small[:, 312:336].rearrange("p (a t h) -> p a t h", a=2, t=TILES)
        lt = small[:, 336:360].rearrange("p (a t h) -> p a t h", a=2, t=TILES)
        csum = small[:, 360:408].rearrange("p (k a t h) -> p k a t h", k=2, a=2, t=TILES)
        rr = small[:, 408:432].rearrange("p (a t h) -> p a t h", a=2, t=TILES)
        mxr, mxl, mra = small[:, 432:436], small[:, 436:440], small[:, 440:444]
        se = small[:, 444:460].rearrange("p (k h) -> p k h", k=4)
        dn = small[:, 460:468].rearrange("p (k h) -> p k h", k=2)
        zero4 = small[:, 468:472]
        idx_slot = sb("idx_slot", 2 * SLOTS, u32).rearrange("p (a s) -> p a s", a=2)
        dots = small[:, 472:488].rearrange("p (a s) -> p a s", a=2)
        coefs = small[:, 488:504].rearrange("p (a s) -> p a s", a=2)
        gmax = small[:, 504:512]
        cond_raw = sig_c

        tops = states[:, 0:256].rearrange("p (b k) -> p b k", b=16)
        ixs_u = states[:, 256:512].bitcast(u32).rearrange("p (b k) -> p b k", b=16)
        ixs_f = states[:, 512:768].rearrange("p (b k) -> p b k", b=16)
        best = states[:, 768:896].rearrange("p (h k) -> p h k", h=PH)
        pos = states[:, 896:1024].bitcast(u32).rearrange("p (h k) -> p h k", h=PH)
        pos_p = states[:, 1024:1152].bitcast(u32).rearrange("p (h k) -> p h k", h=PH)
        pos_f = states[:, 1152:1280].rearrange("p (h k) -> p h k", h=PH)
        e_a = states[:, 1280:1408].rearrange("p (h k) -> p h k", h=PH)
        e_b = states[:, 1408:1536].rearrange("p (h k) -> p h k", h=PH)
        idx = states[:, 1536:1664].bitcast(u32)
        act_a = states[:, 1664:1792]
        coef = states[:, 1792:1920]

        bank = [ctx.enter_context(nc.psum_tensor(f"bank{i}", [P, 512], f32))[:, :] for i in range(8)]
        mod_dram = nc.dram_tensor("mod_rows", (DEPTH, 2, 6 * DM), f32, kind="Internal").ap()

        jobs = tensor_jobs()
        turn = turns(jobs)
        filled = [sem(f"bank{i}_filled") for i in range(8)]
        emptied = [sem(f"bank{i}_emptied") for i in range(8)]
        loads = weight_loads()
        load_at = {key: i for i, (key, _) in enumerate(loads)}
        slot_loaded = [sem(f"weights{i}_loaded") for i in range(RING)]

        def wait_filled(eng, *job):
            b, k = turn[job]
            eng.wait_ge(filled[b], k + 1)
            return bank[b]

        def wait_emptied(eng, *job):
            b, k = turn[job]
            eng.wait_ge(emptied[b], k + 1)

        def empties(eng, ins, *job):
            b, k = turn[job]
            ins.then_inc(emptied[b], 1)
            eng.wait_ge(emptied[b], k + 1)

        def slot(eng, *key):
            i = load_at[key]
            if eng is not None:
                eng.wait_ge(slot_loaded[i % RING], 16 * (i // RING + 1))
            return ring[:, i % RING, :]

        def n_of(l, t):
            return l * TILES + t

        block = ctx.enter_context(nc.Block())

        @block.sync
        def _(sp):
            sp.dma_start(cst, consts).then_inc(sem("consts_loaded"), 16)
            sp.dma_start(x[:, 0, :], x_prompt[0]).then_inc(sem("x_loaded"), 16)
            sp.dma_start(x[:, 1:3, :], x_sample[0].rearrange("(t p) d -> p t d", p=P)).then_inc(sem("x_loaded"), 16)

            def load(key):
                i = load_at[key]
                if i >= RING:
                    wait_filled(sp, *loads[i - RING][1])
                dst = ring[:, i % RING, :]
                kind, l = key[0], key[1]
                if kind == "mod":
                    j = key[2]
                    if j >= 2 or l:
                        wait_emptied(sp, "mod", *((l, j - 2) if j >= 2 else (l - 1, 10 + j)))
                    if l and j == 0:
                        sp.wait_ge(sem("x_mixed"), 2 * TILES * l)
                    sp.dma_start(b_stage[:, j % 2, :], b_mod[l, j * 512:(j + 1) * 512].partition_broadcast(2))\
                      .then_inc(sem(f"b_mod{j % 2}_loaded"), 16)
                    src = w_mod[l, :, j * 512:(j + 1) * 512]
                elif kind == "proj":
                    _, s, w = BLOCKS[key[2]]
                    sp.dma_start(dst[:, 0:KC * w].rearrange("p (c n) -> p c n", c=KC),
                                 w_in[l, :, s:s + w].rearrange("(c p) n -> p c n", p=P))\
                      .then_inc(slot_loaded[i % RING], 16)
                    return
                elif kind == "wg":
                    s = C_GATES + key[2] * DM + key[3] * 512
                    src = w_in[l, :, s:s + 512]
                elif kind == "wb":
                    sp.dma_start(dst.rearrange("p (c n) -> p c n", c=4),
                                 w_branch[l, key[2]].rearrange("(c p) n -> p c n", p=P))\
                      .then_inc(slot_loaded[i % RING], 16)
                    return
                elif kind == "out":
                    src = w_out[l, :, key[2] * 512:(key[2] + 1) * 512]
                elif kind == "q":
                    src = peer_wq[l, :, key[2] * 512:(key[2] + 1) * 512]
                else:
                    sp.dma_start(dst[:, 0:16 * PQ].rearrange("p (b d) -> p b d", b=16),
                                 peer_keys[l].rearrange("h a k d -> k (h a) d")).then_inc(slot_loaded[i % RING], 16)
                    return
                sp.dma_start(dst.rearrange("p (c n) -> p c n", c=KC), src.rearrange("(c p) n -> p c n", p=P))\
                  .then_inc(slot_loaded[i % RING], 16)

            with nc.allow_non_contiguous_dma("columns of small vectors"):
                sp.dma_start(cond_raw[:, :, 0], c_ctx.rearrange("(c p) -> p c", p=P)).then_inc(sem("cond_loaded"), 16)
                sp.dma_start(cond_raw[:, :, 1], c[0].rearrange("(c p) -> p c", p=P)).then_inc(sem("cond_loaded"), 16)
            for j in range(12):
                load(("mod", 0, j))
            for l in range(DEPTH):
                for b in range(RING):
                    load(("proj", l, b))
                if l:
                    sp.wait_ge(sem("x_final"), n_of(l - 1, TILES - 1) + 1)
                pl = sem("params_loaded")
                sp.dma_start(gains, attn_qk_gain[l].rearrange("a d -> (a d)").partition_broadcast(P)).then_inc(pl, 16)
                sp.dma_start(cg_bias, mlstm_gate_bias[l].rearrange("a b h -> (a b h)").partition_broadcast(P)).then_inc(pl, 16)
                sp.dma_start(lam_v, diff_lambda[l].rearrange("a d -> (a d)").partition_broadcast(P)
                             .rearrange("p (a b d) -> p a b d", a=2, b=2)).then_inc(pl, 16)
                sp.dma_start(gn, mlstm_gn[l].rearrange("h d -> (h d)").partition_broadcast(P)).then_inc(pl, 16)
                sp.dma_start(dgn, diff_gn[l].rearrange("h d -> (h d)").partition_broadcast(P)).then_inc(pl, 16)
                with nc.allow_non_contiguous_dma("columns of small vectors"):
                    sp.dma_start(b_bias, gmlp_b[l].rearrange("g p -> p g")).then_inc(pl, 16)
                    for a in range(2):
                        sp.dma_start(c_state[:, a, :, CD], state_c_n[0, l, a].rearrange("h d -> d h")).then_inc(pl, 16)
                sp.dma_start(ws_raw, gmlp_ws[l].rearrange("g p q -> p g q")).then_inc(pl, 16)
                sp.dma_start(m_lat.rearrange("p a h -> p (a h)"),
                             state_c_m[0, l].rearrange("a h -> (a h)").partition_broadcast(P)).then_inc(pl, 16)
                sp.dma_start(akv[:, 3, 0:128], cache_a_k[0, l].rearrange("t g d -> t (g d)")).then_inc(pl, 16)
                sp.dma_start(akv[:, 3, 128:256], cache_a_v[0, l].rearrange("t g d -> t (g d)")).then_inc(pl, 16)
                sp.dma_start(dk[:, 3, :], cache_d_k[0, l].rearrange("t h j d -> t (h j d)")).then_inc(pl, 16)
                sp.dma_start(dv[:, 3, :], cache_d_v[0, l].rearrange("t h d -> t (h d)")).then_inc(pl, 16)
                for a in range(2):
                    sp.dma_start(c_state[:, a, :, 0:CD], state_c_C[0, l, a].rearrange("h d e -> d h e")).then_inc(pl, 16)
                for b in range(RING, len(BLOCKS)):
                    load(("proj", l, b))
                for n in MERGE_ORDER:
                    load(("wg", l, n, 0))
                    load(("wb", l, n))
                    load(("wg", l, n, 1))
                wait_filled(sp, "yT", l, 2, TILES - 1)
                sp.wait_ge(sem("mod_stored"), 16 * 12 * (l + 1))
                g1 = sem("gl1_loaded")
                for n in range(2):
                    sp.dma_start(gl1[:, n, :], mod_dram[l, n, 2 * DM:3 * DM].partition_broadcast(P)).then_inc(g1, 16)
                sp.dma_start(gl1[:, 2, :], ln_g[l, 0].partition_broadcast(P)).then_inc(g1, 16)
                sp.dma_start(gl1[:, 3, :], ln_b[l, 0].partition_broadcast(P)).then_inc(g1, 16)
                for hf in range(2):
                    load(("out", l, hf))
                for k in range(4):
                    load(("q", l, k))
                load(("keys", l))
                wait_filled(sp, "q", l, 2 * PH - 1)
                wait_filled(sp, "h2", l, TILES - 1, 1)
                g2 = sem("gl2_loaded")
                sp.dma_start(gl2[:, 0, :], mod_dram[l, 0, 5 * DM:6 * DM].partition_broadcast(P)).then_inc(g2, 16)
                sp.dma_start(gl2[:, 1, :], ln_g[l, 1].partition_broadcast(P)).then_inc(g2, 16)
                sp.dma_start(gl2[:, 2, :], ln_b[l, 1].partition_broadcast(P)).then_inc(g2, 16)
                sp.wait_ge(sem("x_final"), n_of(l, 0) + 1)
                sp.dma_start(gl2[:, 0, :], mod_dram[l, 1, 5 * DM:6 * DM].partition_broadcast(P)).then_inc(g2, 16)
                if l + 1 < DEPTH:
                    for j in range(12):
                        load(("mod", l + 1, j))
            sp.wait_ge(sem("x_final"), n_of(DEPTH - 1, 0) + 1)
            sp.dma_start(y_prompt[0], x[:, 0, :]).then_inc(sem("y_stored"), 16)
            for t in (1, 2):
                sp.wait_ge(sem("x_final"), n_of(DEPTH - 1, t) + 1)
                sp.dma_start(y_sample[0, (t - 1) * P:t * P, :], x[:, t, :]).then_inc(sem("y_stored"), 16)
            sp.wait_ge(sem("y_stored"), 48)

        @block.tensor
        def _(pe):
            at = [0]

            def begin(*job):
                assert jobs[at[0]] == job, (jobs[at[0]], job)
                at[0] += 1
                b, k = turn[job]
                if k:
                    pe.wait_ge(emptied[b], k)
                return bank[b]

            def done(ins, *job):
                ins.then_inc(filled[turn[job][0]], 1)

            def transposes(job, srcs):
                out = begin(*job)
                for i, s in enumerate(srcs):
                    last = pe.transpose(out[:, i * P:(i + 1) * P], s, ident)
                done(last, *job)

            def modulation(l):
                for j in range(12):
                    out = begin("mod", l, j)
                    w = slot(pe, "mod", l, j).rearrange("p (c n) -> p c n", c=KC)
                    for k in range(KC):
                        last = pe.matmul(out[0:2, :], silu_c[:, k, :], w[:, k, :], start=k == 0, stop=k == KC - 1)
                    done(last, "mod", l, j)
                    if j // 2 in (0, 1, 3, 4):
                        out = begin("mcol", l, j)
                        wait_emptied(pe, "mod", l, j)
                        for i in range(4):
                            last = pe.matmul(out[:, 2 * i:2 * i + 2], m_stage[:, j % 2, i * P:(i + 1) * P],
                                             ident[0:2, 0:2], start=True, stop=True)
                        done(last, "mcol", l, j)

            pe.wait_ge(sem("consts_loaded"), 16)
            pe.wait_ge(sem("silu_ready"), 1)
            modulation(0)
            for l in range(DEPTH):
                if l == 0:
                    pe.wait_ge(sem("x_loaded"), 32)
                for t in range(TILES):
                    if l:
                        pe.wait_ge(sem("x_final"), n_of(l - 1, t) + 1)
                    for hf in range(2):
                        transposes(("xT", l, t, hf), [x[:, t, (4 * hf + i) * P:(4 * hf + i + 1) * P] for i in range(4)])
                def project(b, t):
                    w = BLOCKS[b][2]
                    wt = slot(pe, "proj", l, b)[:, 0:KC * w].rearrange("p (c n) -> p c n", c=KC)
                    if b == 0:
                        wait_emptied(pe, "xT", l, t, 1)
                    out = begin("proj", l, b, t)
                    for k in range(KC):
                        last = pe.matmul(out[:, 0:w], hT[:, k, t * P:(t + 1) * P], wt[:, k, :],
                                         start=k == 0, stop=k == KC - 1)
                    done(last, "proj", l, b, t)

                def merge(n, j):
                    if j == 0:
                        for t in range(TILES):
                            wait_emptied(pe, "yT", l, n, t)
                    wg = slot(pe, "wg", l, n, j // 4).rearrange("p (c n) -> p c n", c=KC)
                    out = begin("gate", l, n, j)
                    for k in range(KC):
                        last = pe.matmul(out[:, 0:T], wg[:, k, (j % 4) * P:(j % 4 + 1) * P], hT[:, k, :],
                                         start=k == 0, stop=k == KC - 1)
                    done(last, "gate", l, n, j)
                    wb = slot(pe, "wb", l, n).rearrange("p (c n) -> p c n", c=4)
                    out = begin("br", l, n, j)
                    for k in range(4):
                        last = pe.matmul(out[:, 0:T], wb[:, k, j * P:(j + 1) * P], yT[n][:, k, :],
                                         start=k == 0, stop=k == 3)
                    done(last, "br", l, n, j)

                def y_transposed(n):
                    for t in range(TILES):
                        transposes(("yT", l, n, t), [ys[n][:, t, i * P:(i + 1) * P] for i in range(4)])

                for b in range(FIRST_BLOCKS):
                    for t in range(TILES):
                        project(b, t)
                pe.wait_ge(sem("params_loaded"), 16 * N_PARAMS * (l + 1))
                transposes(("wsT", l), [ws_raw[:, g, :] for g in range(BG)])

                for t in range(TILES):
                    pe.wait_ge(sem("qa_ready"), n_of(l, t) + 1)
                    transposes(("qTA", l, t), [aq[:, t, i * P:(i + 1) * P] for i in range(4)])
                pe.wait_ge(sem("ka_ready"), l + 1)
                for s in range(4):
                    transposes(("kTA", l, s), [k_dup[:, s, g, :] for g in range(AG)])
                for t in range(TILES):
                    wait_emptied(pe, "qTA", l, t)
                for s in range(4):
                    wait_emptied(pe, "kTA", l, s)
                n_a = len(A_UNITS)
                for i in range(n_a + LAG_V):
                    if i < n_a:
                        t, h = A_UNITS[i]
                        k0, nk = KEY_SLOTS[t][0] * P, len(KEY_SLOTS[t]) * P
                        half = slice(64 * (h % 2), 64 * (h % 2) + 64)
                        out = begin("sA", l, i)
                        done(pe.matmul(out[:, 0:nk], qTA[half, h // 2, t * P:(t + 1) * P],
                                       kTA[half, h // (AH // AG), k0:k0 + nk], start=True, stop=True), "sA", l, i)
                    if 0 <= i - LAG_T < n_a:
                        u = i - LAG_T
                        wait_emptied(pe, "sA", l, u)
                        transposes(("pTA", l, u), [pr[:, u % 6, j * P:(j + 1) * P]
                                                   for j in range(len(KEY_SLOTS[A_UNITS[u][0]]))])
                    if i >= LAG_V:
                        u = i - LAG_V
                        t, h = A_UNITS[u]
                        g = h // (AH // AG)
                        out = begin("oA", l, t) if h == 0 else bank[turn["oA", l, t][0]]
                        wait_emptied(pe, "pTA", l, u)
                        ks = KEY_SLOTS[t]
                        for j, s in enumerate(ks):
                            last = pe.matmul(out[:, h * AD:(h + 1) * AD], pt[:, u % 2, j * P:(j + 1) * P],
                                             akv[:, TILE_OF_KEY_SLOT[s], 128 + g * AD:128 + (g + 1) * AD],
                                             start=j == 0, stop=j == len(ks) - 1)
                        last.then_inc(sem("a_values_done"), 1)
                    if i in A_FILL:
                        project(*A_FILL[i])

                for t in range(TILES):
                    pe.wait_ge(sem("qd_ready"), n_of(l, t) + 1)
                    transposes(("qTD", l, t), [dq[:, t, i * P:(i + 1) * P] for i in range(4)])
                for s in range(4):
                    transposes(("kTD", l, s), [dk[:, TILE_OF_KEY_SLOT[s], i * P:(i + 1) * P] for i in range(4)])
                for t in range(TILES):
                    wait_emptied(pe, "qTD", l, t)
                for s in range(4):
                    wait_emptied(pe, "kTD", l, s)
                n_d = len(D_UNITS)
                for i in range(n_d + LAG_V):
                    if i < n_d:
                        t, h = D_UNITS[i]
                        k0, nk = KEY_SLOTS[t][0] * P, len(KEY_SLOTS[t]) * P
                        for j in range(2):
                            half = slice(64 * j, 64 * j + 64)
                            out = begin("sD", l, i, j)
                            done(pe.matmul(out[:, 0:nk], qTD[half, h, t * P:(t + 1) * P],
                                           kTD[half, h, k0:k0 + nk], start=True, stop=True), "sD", l, i, j)
                    if 0 <= i - LAG_T < n_d:
                        u = i - LAG_T
                        pe.wait_ge(sem("d_combined"), l * n_d + u + 1)
                        transposes(("pTD", l, u), [pr[:, (2 * u) % 6, j * P:(j + 1) * P]
                                                   for j in range(len(KEY_SLOTS[D_UNITS[u][0]]))])
                    if i >= LAG_V:
                        u = i - LAG_V
                        t, h = D_UNITS[u]
                        out = begin("oD", l, t) if h == 0 else bank[turn["oD", l, t][0]]
                        wait_emptied(pe, "pTD", l, u)
                        ks = KEY_SLOTS[t]
                        for j, s in enumerate(ks):
                            last = pe.matmul(out[:, h * DV:(h + 1) * DV], pt[:, u % 2, j * P:(j + 1) * P],
                                             dv[:, TILE_OF_KEY_SLOT[s], h * DV:(h + 1) * DV],
                                             start=j == 0, stop=j == len(ks) - 1)
                        last.then_inc(sem("d_values_done"), 1)
                    if i in D_FILL:
                        project(*D_FILL[i])
                for b, t in LAST_FILL:
                    project(b, t)

                wait_emptied(pe, "wsT", l)
                for t in range(TILES):
                    pe.wait_ge(sem("vn_ready"), n_of(l, t) + 1)
                    out = begin("bmm", l, t)
                    for g in range(BG):
                        last = pe.matmul(out[:, g * P:(g + 1) * P], wsT[:, g, :], bv[:, t, g * P:(g + 1) * P],
                                         start=True, stop=True)
                    done(last, "bmm", l, t)

                for t in range(TILES):
                    wait_emptied(pe, "proj", l, BLK["cq"], t)
                    wait_emptied(pe, "proj", l, BLK["ck"], t)
                for t in range(TILES):
                    transposes(("qTC", l, t), [cq[:, t, i * P:(i + 1) * P] for i in range(4)])
                for t in range(TILES):
                    transposes(("kTC", l, t), [ck[:, t, i * P:(i + 1) * P] for i in range(4)])
                for t in range(TILES):
                    wait_emptied(pe, "qTC", l, t)
                    wait_emptied(pe, "kTC", l, t)
                    out = begin("sC", l, t)
                    for h in range(CH):
                        last = pe.matmul(out[:, h * P:(h + 1) * P], qTC[:, h, t * P:(t + 1) * P],
                                         kTC[:, h, t * P:(t + 1) * P], start=True, stop=True)
                    done(last, "sC", l, t)
                for n, kind in ((0, "oA"), (1, "bmm")):
                    for t in range(TILES):
                        wait_emptied(pe, kind, l, t)
                    y_transposed(n)
                pe.wait_ge(sem("lf_ready"), l + 1)
                out = begin("cum", l)
                for a in range(2):
                    pe.matmul(out[:, 12 * a:12 * a + 12], tri[:, a, :], lf[:, a].rearrange("p t h -> p (t h)"),
                              start=True, stop=True)
                done(pe.matmul(out[:, 24:48], ones, lf.rearrange("p a t h -> p (a t h)"), start=True, stop=True),
                     "cum", l)
                pe.wait_ge(sem("yd_ready"), l + 1)
                y_transposed(3)
                for u, (t, a) in enumerate(C_UNITS):
                    nu = l * len(C_UNITS) + u
                    pe.wait_ge(sem("diag_ready"), nu + 1)
                    out = begin("rb", l, u)
                    done(pe.matmul(out, ones, diag.rearrange("p h s -> p (h s)"), start=True, stop=True), "rb", l, u)
                    for n, j in C_FILL[2 * u]:
                        merge(n, j)
                    pe.wait_ge(sem("w_ready"), nu + 1)
                    transposes(("wT", l, u), [Wc[:, h, :] for h in range(CH)])
                    if u in C_UPDATES:
                        pe.wait_ge(sem("kws_ready"), l * len(C_UPDATES) + u + 1)
                        for p2 in range(2):
                            out = begin("kv", l, u, p2)
                            for h in (2 * p2, 2 * p2 + 1):
                                o = 256 * (h % 2)
                                last = pe.matmul(out[:, o:o + CD + 1], kws[:, h, :], cv[:, t, h, :],
                                                 start=True, stop=True)
                            done(last, "kv", l, u, p2)
                    wait_emptied(pe, "wT", l, u)
                    for p2 in range(2):
                        out = begin("num", l, u, p2)
                        for h in (2 * p2, 2 * p2 + 1):
                            o = 256 * (h % 2)
                            last = pe.matmul(out[:, o:o + CD + 1], WT[:, h, :], cv[:, t, h, :], start=True, stop=True)
                        done(last, "num", l, u, p2)
                    if t:
                        if u >= 4:
                            pe.wait_ge(sem("state_ready"), 2 * l + u - 3)
                        for p2 in range(2):
                            out = begin("qC", l, u, p2)
                            for h in (2 * p2, 2 * p2 + 1):
                                o = 256 * (h % 2)
                                last = pe.matmul(out[:, o:o + CD + 1], qTC[:, h, t * P:(t + 1) * P],
                                                 c_state[:, a, h, :], start=True, stop=True)
                            done(last, "qC", l, u, p2)

                    for n, j in C_FILL[2 * u + 1]:
                        merge(n, j)
                pe.wait_ge(sem("yc_ready"), l + 1)
                y_transposed(2)
                for n, j in LAST_MERGES:
                    merge(n, j)
                pe.wait_ge(sem("merged_ready"), l + 1)
                for hf in range(2):
                    wo = slot(pe, "out", l, hf).rearrange("p (c n) -> p c n", c=KC)
                    for t in range(TILES):
                        out = begin("out", l, hf, t)
                        for k in range(KC):
                            last = pe.matmul(out, merged[:, k, t * P:(t + 1) * P], wo[:, k, :],
                                             start=k == 0, stop=k == KC - 1)
                        done(last, "out", l, hf, t)

                for t in range(TILES):
                    pe.wait_ge(sem("x_mid"), n_of(l, t) + 1)
                    for hf in range(2):
                        transposes(("x2T", l, t, hf), [x[:, t, (4 * hf + i) * P:(4 * hf + i + 1) * P] for i in range(4)])
                for t in range(TILES):
                    for hf in range(2):
                        wait_emptied(pe, "x2T", l, t, hf)
                        transposes(("h2", l, t, hf), [hT[:, 4 * hf + i, t * P:(t + 1) * P] for i in range(4)])
                for j in range(2 * PH):
                    wq = slot(pe, "q", l, j // 4).rearrange("p (c n) -> p c n", c=KC)
                    out = begin("q", l, j)
                    for k in range(KC):
                        last = pe.matmul(out[:, 0:T], wq[:, k, (j % 4) * P:(j % 4 + 1) * P], hT[:, k, :],
                                         start=k == 0, stop=k == KC - 1)
                    done(last, "q", l, j)
                keys = slot(pe, "keys", l)[:, 0:16 * PQ].rearrange("p (b d) -> p b d", b=16)
                for i in range(4):
                    transposes(("kT", l, i), [keys[:, 4 * i + k, :] for k in range(4)])
                for i in range(4):
                    wait_emptied(pe, "kT", l, i)
                for j in range(2 * PH):
                    wait_emptied(pe, "q", l, j)
                for t in range(TILES):
                    for i in range(4):
                        out = begin("sc", l, t, i)
                        for k in range(4):
                            last = pe.matmul(out[:, k * P:(k + 1) * P], qTp[:, 4 * i + k, t * P:(t + 1) * P],
                                             keysT[:, 4 * i + k, :], start=True, stop=True)
                        done(last, "sc", l, t, i)
                if l + 1 < DEPTH:
                    modulation(l + 1)
            assert at[0] == len(jobs)

        @block.scalar
        def _(act):
            steps = [0]

            def step(ins):
                ins.then_inc(sem("act_steps"), 1)
                steps[0] += 1
                act.wait_ge(sem("act_steps"), steps[0])

            def copy_out(job, dst, width=512, scale=None):
                src = wait_filled(act, *job)[:, 0:width]
                if len(dst.shape) == 3:
                    src = src.rearrange("p (a b) -> p a b", a=dst.shape[1])
                if scale is None:
                    empties(act, act.copy(dst, src), *job)
                else:
                    empties(act, act.mul(dst, src, scale), *job)

            act.wait_ge(sem("cond_loaded"), 32)
            act.activation(silu_c, cond_raw, ACT.Sigmoid).then_inc(sem("cond_sigmoid"), 1)
            for l in range(DEPTH):
                def project(b, t):
                    name, _, w = BLOCKS[b]
                    job = ("proj", l, b, t)
                    if name == "cg":
                        copy_out(job, cg[:, t, :], 16)
                    elif name == "ck":
                        copy_out(job, ck[:, t, :], 512, CD ** -0.5)
                    elif name == "cv":
                        copy_out(job, cv[:, t, :, 0:CD])
                    elif name == "co":
                        src = wait_filled(act, *job)
                        empties(act, act.activation(co[:, t, :], src, ACT.Sigmoid), *job)
                    else:
                        copy_out(job, {"aq": aq, "akv": akv, "dq": dq, "dk": dk, "dv": dv, "bu": bu,
                                       "bv": bv, "cq": cq}[name][:, t, :], w)

                def merge(n, j):
                    at = MERGES.index((n, j))
                    src = wait_filled(act, "gate", l, n, j)
                    if at >= 2:
                        act.wait_ge(sem("sg_used"), l * len(MERGES) + at - 1)
                    empties(act, act.activation(sg[:, j % 2, :], src[:, 0:T], ACT.Sigmoid), "gate", l, n, j)

                for b in range(FIRST_BLOCKS):
                    for t in range(TILES):
                        project(b, t)
                copy_out(("wsT", l), wsT)
                for t in range(TILES):
                    copy_out(("qTA", l, t), qTA[:, :, t * P:(t + 1) * P])
                for s in range(4):
                    copy_out(("kTA", l, s), kTA[:, :, s * P:(s + 1) * P], 256)
                n_a = len(A_UNITS)
                for i in range(n_a):
                    t, h = A_UNITS[i]
                    nk = len(KEY_SLOTS[t]) * P
                    if i >= 6:
                        wait_filled(act, "pTA", l, i - 6)
                    act.wait_ge(sem("a_negmax"), l * n_a + i + 1)
                    src = wait_filled(act, "sA", l, i)
                    step(act.activation(pr[:, i % 6, 0:nk], src[:, 0:nk], ACT.Exp, bias=negm[:, i:i + 1],
                                        scale=AD ** -0.5, accum_out=sums[:, i:i + 1]))
                    act.sem_inc(emptied[turn["sA", l, i][0]], 1)
                    if i in A_FILL:
                        project(*A_FILL[i])
                for i in range(n_a, n_a + LAG_V):
                    if i in A_FILL:
                        project(*A_FILL[i])
                for t in range(TILES):
                    copy_out(("qTD", l, t), qTD[:, :, t * P:(t + 1) * P])
                for s in range(4):
                    copy_out(("kTD", l, s), kTD[:, :, s * P:(s + 1) * P])
                act.wait_ge(sem("lam_sums"), l + 1)
                step(act.activation(lam_e, lam_e, ACT.Exp))
                act.sem_inc(sem("lam_exps"), 1)
                n_d = len(D_UNITS)
                for i in range(n_d + LAG_T):
                    if i < n_d:
                        t, h = D_UNITS[i]
                        nk = len(KEY_SLOTS[t]) * P
                        if i >= 3:
                            wait_filled(act, "pTD", l, i - 3)
                        else:
                            wait_filled(act, "pTA", l, n_a - 1)
                        for j in range(2):
                            act.wait_ge(sem("d_negmax"), 2 * (l * n_d + i) + j + 1)
                            src = wait_filled(act, "sD", l, i, j)
                            step(act.activation(pr[:, (2 * i + j) % 6, 0:nk], src[:, 0:nk], ACT.Exp,
                                                bias=negm[:, 2 * i + j:2 * i + j + 1], scale=DD ** -0.5,
                                                accum_out=sums[:, 2 * i + j:2 * i + j + 1]))
                            act.sem_inc(emptied[turn["sD", l, i, j][0]], 1)
                    if i >= LAG_T:
                        u = i - LAG_T
                        nk = len(KEY_SLOTS[D_UNITS[u][0]]) * P
                        if u >= 2:
                            act.wait_ge(sem("d_values_done"), l * n_d + u - 1)
                        else:
                            act.wait_ge(sem("a_values_done"), (l + 1) * n_a)
                        copy_out(("pTD", l, u), pt[:, u % 2, 0:nk], nk)
                    if i in D_FILL:
                        project(*D_FILL[i])
                for b, t in LAST_FILL:
                    project(b, t)
                for t in range(TILES):
                    copy_out(("qTC", l, t), qTC[:, :, t * P:(t + 1) * P])
                for t in range(TILES):
                    copy_out(("kTC", l, t), kTC[:, :, t * P:(t + 1) * P])
                for t in range(TILES):
                    copy_out(("sC", l, t), sC[:, t, :])
                for n in (0, 1):
                    for t in range(TILES):
                        copy_out(("yT", l, n, t), yT[n][:, :, t * P:(t + 1) * P])
                act.wait_ge(sem("lf_abs"), l + 1)
                step(act.activation(lt, lt, ACT.Exp, scale=-1.0))
                step(act.activation(lt, lt, ACT.Ln, bias=1.0))
                act.sem_inc(sem("lf_log"), 1)
                for t in range(TILES):
                    copy_out(("yT", l, 3, t), yT[3][:, :, t * P:(t + 1) * P])
                for u, (t, a) in enumerate(C_UNITS):
                    nu = l * len(C_UNITS) + u
                    act.wait_ge(sem("exp_args"), nu + 1)
                    act.activation(se, se, ACT.Exp)
                    step(act.activation(Mx, Mx, ACT.Exp))
                    act.sem_inc(sem("exps_ready"), 1)
                    for n, j in C_FILL[2 * u]:
                        merge(n, j)
                    copy_out(("wT", l, u), WT)
                    if u < 2:
                        for p2 in range(2):
                            src = wait_filled(act, "kv", l, u, p2).rearrange("p (h e) -> p h e", h=2)[:, :, 0:CD + 1]
                            empties(act, act.copy(c_new[:, a, 2 * p2:2 * p2 + 2, :], src), "kv", l, u, p2)
                        act.sem_inc(sem("c_new_ready"), 1)
                    if u:
                        act.wait_ge(sem("nd_used"), nu)
                    for p2 in range(2):
                        src = wait_filled(act, "num", l, u, p2).rearrange("p (h e) -> p h e", h=2)[:, :, 0:CD + 1]
                        empties(act, act.copy(ND[:, 2 * p2:2 * p2 + 2, :], src), "num", l, u, p2)
                    for n, j in C_FILL[2 * u + 1]:
                        merge(n, j)
                for t in range(TILES):
                    copy_out(("yT", l, 2, t), yT[2][:, :, t * P:(t + 1) * P])
                for n, j in LAST_MERGES:
                    merge(n, j)
                act.wait_ge(sem("kv_stored"), 64 * (l + 1))
                for t in range(TILES):
                    for hf in range(2):
                        copy_out(("h2", l, t, hf), h2[:, t, hf * 512:(hf + 1) * 512])
                for j in range(2 * PH):
                    copy_out(("q", l, j), qTp[:, j, :], T)
                for i in range(4):
                    copy_out(("kT", l, i), keysT[:, 4 * i:4 * i + 4, :])
                for t in range(TILES):
                    n = n_of(l, t)
                    if t:
                        act.wait_ge(sem("scores_used"), n)
                    for i in range(4):
                        copy_out(("sc", l, t, i), S[:, 4 * i:4 * i + 4, :])
                    act.wait_ge(sem("gate_args"), n + 1)
                    step(act.activation(best, best, ACT.Exp))
                    act.sem_inc(sem("gate_exps"), 1)
                    act.wait_ge(sem("dots_ready"), n + 1)
                    step(act.activation(act_a, act_a, ACT.Gelu))
                    act.sem_inc(sem("gelu_ready"), 1)

        @block.vector
        def _(v):
            steps = [0]

            def step(ins):
                ins.then_inc(sem("vec_steps"), 1)
                steps[0] += 1
                v.wait_ge(sem("vec_steps"), steps[0])

            roots = [0]

            def inv_sqrt(n):
                v.sem_inc(sem("squares_ready"), 1)
                roots[0] += 1
                v.wait_ge(sem("roots_ready"), roots[0])

            def bc(ap, shape, axis):
                return ap.unsqueeze(axis).to_broadcast(shape)

            def rope(src, n, t):
                s5 = src.rearrange("p (n a b c) -> p n a b c", n=n, a=2, b=2)
                t5 = tmp[:, 0:n * 64].rearrange("p (n a b c) -> p n a b c", n=n, a=2, b=2)
                sn = rope_cs[:, 1, t, :].rearrange("p (a b c) -> p a b c", a=2, b=2)
                for b in range(2):
                    last = v.tensor_tensor(t5[:, :, :, b, :], s5[:, :, :, 1 - b, :],
                                           bc(sn[:, :, b, :], [P, n, 2, 16], 1), ALU.mult)
                step(last)
                s3 = src.rearrange("p (n d) -> p n d", n=n)
                step(v.tensor_tensor(s3, s3, bc(rope_cs[:, 0, t, :], [P, n, 64], 1), ALU.mult))
                step(v.tensor_tensor(src, src, tmp[:, 0:n * 64], ALU.add))

            def rms_heads(src, n, d):
                s3 = src.rearrange("p (n d) -> p n d", n=n)
                step(v.tensor_tensor(tmp[:, 0:n * d], src, src, ALU.mult))
                step(v.tensor_reduce(ms[:, 0:n], tmp[:, 0:n * d].rearrange("p (n d) -> p n d", n=n), X, ALU.add))
                step(v.tensor_scalar(ms[:, 0:n], ms[:, 0:n], 1.0 / d, EPS, ALU.mult, ALU.add))
                inv_sqrt(n)
                step(v.tensor_tensor(s3, s3, bc(rs[:, 0:n], [P, n, d], 2), ALU.mult))

            def modulate(job, l, t, hf, which):
                src = wait_filled(v, *job)
                cond = 0 if t == 0 else 1
                for i in range(4):
                    k = 4 * hf + i
                    last = v.tensor_scalar(hT[:, k, t * P:(t + 1) * P], src[:, i * P:(i + 1) * P],
                                           modcol[:, l, which + 1, k, cond:cond + 1],
                                           modcol[:, l, which, k, cond:cond + 1], ALU.mult, ALU.add)
                empties(v, last, *job)

            def modulation(l):
                for j in range(12):
                    src = wait_filled(v, "mod", l, j)
                    v.wait_ge(sem(f"b_mod{j % 2}_loaded"), 16 * (6 * l + j // 2 + 1))
                    if j >= 2 or l:
                        v.wait_ge(sem(f"mod_stored{j % 2}"), 16 * (6 * l + j // 2))
                        jj, ll = (j - 2, l) if j >= 2 else (10 + j, l - 1)
                        if jj // 2 in (0, 1, 3, 4):
                            wait_filled(v, "mcol", ll, jj)
                    empties(v, v.tensor_tensor(m_stage[:, j % 2, :], src[0:2, :], b_stage[:, j % 2, :], ALU.add),
                            "mod", l, j)
                    v.sem_inc(sem("mod_row"), 1)
                    if j // 2 in (0, 1, 3, 4):
                        src = wait_filled(v, "mcol", l, j)
                        a = {0: 0, 1: 1, 3: 2, 4: 3}[j // 2]
                        dst = modcol[:, l, a, 4 * (j % 2):4 * (j % 2) + 4, :].rearrange("p c n -> p (c n)")
                        add = 1.0 if a % 2 else 0.0
                        empties(v, v.tensor_scalar(dst, src[:, 0:8], add, None, ALU.add), "mcol", l, j)

            def layer_norm(xt, lg, lb):
                for i in range(2):
                    last = v.bn_stats(stats[:, i, :], xt[:, i * 512:(i + 1) * 512])
                step(last)
                step(v.bn_aggr(aggr[:, 0, :], stats[:, 0:2, :].rearrange("p a s -> p (a s)")))
                step(v.tensor_scalar(ms[:, 0:1], aggr[:, 0, 1:2], EPS, None, ALU.add))
                inv_sqrt(1)
                step(v.tensor_scalar(xt, xt, aggr[:, 0, 0:1], rs[:, 0:1], ALU.subtract, ALU.mult))
                step(v.tensor_tensor(xt, xt, lg, ALU.mult))
                step(v.tensor_tensor(xt, xt, lb, ALU.add))

            v.memset(small[:, 468:472], 0.0)
            v.wait_ge(sem("cond_sigmoid"), 1)
            v.tensor_tensor(silu_c, silu_c, cond_raw, ALU.mult).then_inc(sem("silu_ready"), 1)
            v.wait_ge(sem("consts_loaded"), 16)
            modulation(0)
            for l in range(DEPTH):
                lam_init = 0.8 - 0.6 * math.exp(-0.3 * l)
                for t in range(TILES):
                    for hf in range(2):
                        modulate(("xT", l, t, hf), l, t, hf, 0)
                step(v.memset(cv[:, :, :, CD], 1.0))
                v.wait_ge(sem("params_loaded"), 16 * N_PARAMS * (l + 1))
                step(v.tensor_tensor(tmp[:, 0:128].rearrange("p (a d) -> p a d", a=2), lam_v[:, :, 0, :],
                                     lam_v[:, :, 1, :], ALU.mult))
                step(v.tensor_reduce(lam_e, tmp[:, 0:128].rearrange("p (a d) -> p a d", a=2), X, ALU.add))
                v.sem_inc(sem("lam_sums"), 1)

                for t in range(TILES):
                    wait_emptied(v, "proj", l, BLK["aq"], t)
                    rms_heads(aq[:, t, :], AH, AD)
                    q3 = aq[:, t, :].rearrange("p (n d) -> p n d", n=AH)
                    step(v.tensor_tensor(q3, q3, bc(gains[:, 0, :], [P, AH, AD], 1), ALU.mult))
                    if t:
                        rope(aq[:, t, :], AH, t - 1)
                    v.sem_inc(sem("qa_ready"), 1)
                for t in range(TILES):
                    wait_emptied(v, "proj", l, BLK["akv"], t)
                    ak = akv[:, t, 0:128]
                    rms_heads(ak, AG, AD)
                    k3 = ak.rearrange("p (n d) -> p n d", n=AG)
                    step(v.tensor_tensor(k3, k3, bc(gains[:, 1, :], [P, AG, AD], 1), ALU.mult))
                    if t:
                        rope(ak, AG, t - 1)
                    else:
                        v.sem_inc(sem("ak_ready"), 1)
                for s in range(4):
                    k3 = akv[:, TILE_OF_KEY_SLOT[s], 0:128].rearrange("p (g d) -> p g d", g=AG)
                    for r in range(2):
                        last = v.tensor_copy(k_dup[:, s, :, r * 64:(r + 1) * 64], k3)
                step(last)
                v.sem_inc(sem("ka_ready"), 1)
                for t in range(TILES):
                    wait_emptied(v, "proj", l, BLK["dq"], t)
                    wait_emptied(v, "proj", l, BLK["dk"], t)
                    if t:
                        rope(dq[:, t, :], 8, t - 1)
                        rope(dk[:, t, :], 8, t - 1)
                    v.sem_inc(sem("qd_ready"), 1)
                n_a = len(A_UNITS)
                for i in range(n_a + LAG_V):
                    if i < n_a:
                        nk = len(KEY_SLOTS[A_UNITS[i][0]]) * P
                        src = wait_filled(v, "sA", l, i)
                        step(v.reduce_max(negm[:, i:i + 1], src[:, 0:nk], X))
                        v.tensor_scalar(negm[:, i:i + 1], negm[:, i:i + 1], -(AD ** -0.5), None, ALU.mult)\
                         .then_inc(sem("a_negmax"), 1)
                    if 0 <= i - LAG_T < n_a:
                        u = i - LAG_T
                        nk = len(KEY_SLOTS[A_UNITS[u][0]]) * P
                        src = wait_filled(v, "pTA", l, u)
                        if u >= 2:
                            v.wait_ge(sem("a_values_done"), l * n_a + u - 1)
                        empties(v, v.tensor_copy(pt[:, u % 2, 0:nk], src[:, 0:nk]), "pTA", l, u)
                    if i >= LAG_V and A_UNITS[i - LAG_V][1] == AH - 1:
                        t = A_UNITS[i - LAG_V][0]
                        v.wait_ge(sem("a_values_done"), l * n_a + (t + 1) * AH)
                        src = bank[turn["oA", l, t][0]]
                        step(v.reciprocal(rsum[:, 0:AH], sums[:, t * AH:(t + 1) * AH]))
                        empties(v, v.tensor_tensor(yA[:, t, :].rearrange("p (h d) -> p h d", h=AH),
                                                   src.rearrange("p (h d) -> p h d", h=AH),
                                                   bc(rsum[:, 0:AH], [P, AH, AD], 2), ALU.mult), "oA", l, t)

                v.wait_ge(sem("lam_exps"), l + 1)
                step(v.tensor_tensor(neg_lam, lam_e[:, 1:2], lam_e[:, 0:1], ALU.subtract))
                step(v.tensor_scalar(neg_lam, neg_lam, -lam_init, None, ALU.add))
                n_d = len(D_UNITS)
                for i in range(n_d + LAG_V):
                    if i < n_d:
                        nk = len(KEY_SLOTS[D_UNITS[i][0]]) * P
                        for j in range(2):
                            src = wait_filled(v, "sD", l, i, j)
                            m = negm[:, 2 * i + j:2 * i + j + 1]
                            step(v.reduce_max(m, src[:, 0:nk], X))
                            v.tensor_scalar(m, m, -(DD ** -0.5), None, ALU.mult).then_inc(sem("d_negmax"), 1)
                    if 0 <= i - 1 < n_d:
                        u = i - 1
                        nk = len(KEY_SLOTS[D_UNITS[u][0]]) * P
                        wait_emptied(v, "sD", l, u, 0)
                        wait_emptied(v, "sD", l, u, 1)
                        r = rsum[:, 0:2]
                        step(v.reciprocal(r, sums[:, 2 * u:2 * u + 2]))
                        step(v.tensor_tensor(r[:, 1:2], r[:, 1:2], neg_lam, ALU.mult))
                        p0, p1 = pr[:, (2 * u) % 6, 0:nk], pr[:, (2 * u + 1) % 6, 0:nk]
                        step(v.tensor_scalar(p0, p0, r[:, 0:1], None, ALU.mult))
                        step(v.scalar_tensor_tensor(out=p0, in0=p1, scalar=r[:, 1:2], in1=p0, op0=ALU.mult,
                                                    op1=ALU.add))
                        v.sem_inc(sem("d_combined"), 1)
                    if i >= LAG_V and D_UNITS[i - LAG_V][1] == DH - 1:
                        t = D_UNITS[i - LAG_V][0]
                        v.wait_ge(sem("d_values_done"), l * n_d + (t + 1) * DH)
                        if t == 0:
                            v.wait_ge(sem("kv_stored"), 64 * (l + 1))
                            for s in range(4):
                                wait_filled(v, "kTD", l, s)
                        empties(v, v.tensor_copy(yD[:, t, :], bank[turn["oD", l, t][0]]), "oD", l, t)
                for t in range(TILES):
                    wait_emptied(v, "proj", l, BLK["bv"], t)
                    step(v.bn_stats(stats[:, 0, :], bv[:, t, :]))
                    step(v.bn_aggr(aggr[:, 0, :], stats[:, 0, :]))
                    step(v.tensor_scalar(ms[:, 0:1], aggr[:, 0, 1:2], EPS, None, ALU.add))
                    inv_sqrt(1)
                    step(v.tensor_scalar(bv[:, t, :], bv[:, t, :], aggr[:, 0, 0:1], rs[:, 0:1],
                                         ALU.subtract, ALU.mult))
                    v.sem_inc(sem("vn_ready"), 1)
                for t in range(TILES):
                    src = wait_filled(v, "bmm", l, t)
                    wait_emptied(v, "proj", l, BLK["bu"], t)
                    for g in range(BG):
                        cols = slice(g * P, (g + 1) * P)
                        last = v.scalar_tensor_tensor(out=yB[:, t, cols], in0=src[:, cols], scalar=b_bias[:, g:g + 1],
                                                      in1=bu[:, t, cols], op0=ALU.add, op1=ALU.mult)
                    empties(v, last, "bmm", l, t)

                for t in range(TILES):
                    rms_heads(yD[:, t, :], DH, DV)
                    step(v.scalar_tensor_tensor(out=yD[:, t, :], in0=yD[:, t, :], scalar=1.0 - lam_init, in1=dgn,
                                                op0=ALU.mult, op1=ALU.mult))

                v.sem_inc(sem("yd_ready"), 1)
                for t in range(TILES):
                    wait_emptied(v, "proj", l, BLK["cg"], t)
                step(v.tensor_tensor(cg, cg, bc(cg_bias, [P, TILES, 16], 1), ALU.add))
                g5 = cg.rearrange("p t (a k h) -> p a k t h", a=2, k=2)
                for a in range(2):
                    last = v.tensor_scalar(lf[:, a], g5[:, a, 1], -1.0, None, ALU.mult)
                step(last)
                for a in range(2):
                    last = v.tensor_tensor(lt[:, a], lf[:, a], g5[:, a, 1], ALU.max)
                step(last)
                v.sem_inc(sem("lf_abs"), 1)
                v.wait_ge(sem("lf_log"), l + 1)
                for a in range(2):
                    last = v.scalar_tensor_tensor(out=lf[:, a], in0=g5[:, a, 1], scalar=0.0, in1=lt[:, a],
                                                  op0=ALU.min, op1=ALU.subtract)
                step(last)
                v.sem_inc(sem("lf_ready"), 1)
                src = wait_filled(v, "cum", l)
                empties(v, v.tensor_copy(csum.rearrange("p k a t h -> p (k a t h)"), src[:, 0:48]), "cum", l)
                for a in range(2):
                    last = v.tensor_tensor(rr[:, a], g5[:, a, 0], csum[:, 0, a], ALU.subtract)
                step(last)
                for t in range(TILES):
                    wait_emptied(v, "sC", l, t)
                    wait_filled(v, "pTD", l, n_d - 1)
                def merge(n, j):
                    wait_emptied(v, "gate", l, n, j)
                    src = wait_filled(v, "br", l, n, j)[:, 0:T]
                    dst = merged[:, j, :] if n == MERGE_ORDER[0] else prod
                    empties(v, v.tensor_tensor(dst, src, sg[:, j % 2, :], ALU.mult), "br", l, n, j)
                    v.sem_inc(sem("sg_used"), 1)
                    if n != MERGE_ORDER[0]:
                        step(v.tensor_tensor(merged[:, j, :], merged[:, j, :], prod, ALU.add))

                def spread(u):
                    t, a = C_UNITS[u]
                    step(v.tensor_tensor(diag, bc(ident, [P, CH, P], 1), bc(rr[:, a, t, :], [P, CH, P], 2),
                                         ALU.mult))
                    v.sem_inc(sem("diag_ready"), 1)

                spread(0)
                for u, (t, a) in enumerate(C_UNITS):
                    nu = l * len(C_UNITS) + u
                    r = rr[:, a, t, :]
                    m = m_lat[:, a, :] if t else zero4
                    src = wait_filled(v, "rb", l, u).rearrange("p (h s) -> p h s", h=CH)
                    step(v.tensor_tensor(Mx, src, bc(negmask[:, a, :], [P, CH, P], 1), ALU.add))
                    v.tensor_reduce(mxr, Mx, X, ALU.max)
                    empties(v, v.tensor_reduce(mra, src, X, ALU.max), "rb", l, u)
                    v.tensor_tensor(mxl, mra, m, ALU.max)
                    step(v.tensor_tensor(mxr, mxr, m, ALU.max))
                    v.tensor_tensor(Mx, Mx, bc(mxr, [P, CH, P], 2), ALU.subtract)
                    v.tensor_tensor(se[:, 0, :], m, mxr, ALU.subtract)
                    v.scalar_tensor_tensor(out=se[:, 1, :], in0=csum[:, 0, a, t, :], scalar=-1.0, in1=mxr,
                                           op0=ALU.mult, op1=ALU.subtract)
                    v.tensor_tensor(se[:, 2, :], m, mxl, ALU.subtract)
                    step(v.tensor_tensor(se[:, 3, :], r, mxl, ALU.subtract))
                    v.sem_inc(sem("exp_args"), 1)
                    if u in C_UPDATES:
                        dst = m_lat[:, a, :] if t else m_out[:, a, :]
                        step(v.tensor_tensor(dst, csum[:, 1, a, t, :], mxl, ALU.add))
                    v.wait_ge(sem("exps_ready"), nu + 1)
                    step(v.tensor_tensor(Wc, sC[:, t, :].rearrange("p (h s) -> p h s", h=CH), Mx, ALU.mult))
                    v.sem_inc(sem("w_ready"), 1)
                    if u in C_UPDATES:
                        step(v.tensor_tensor(kws, ck[:, t, :].rearrange("p (h d) -> p h d", h=CH),
                                             bc(se[:, 3, :], [P, CH, CD], 2), ALU.mult))
                        v.sem_inc(sem("kws_ready"), 1)
                    for n, j in C_FILL[2 * u]:
                        merge(n, j)
                    wait_emptied(v, "num", l, u, 0)
                    wait_emptied(v, "num", l, u, 1)
                    if t:
                        for p2 in range(2):
                            src = wait_filled(v, "qC", l, u, p2)
                            for h in (2 * p2, 2 * p2 + 1):
                                o = 256 * (h % 2)
                                last = v.scalar_tensor_tensor(out=ND[:, h, :], in0=src[:, o:o + CD + 1],
                                                              scalar=se[:, 0, h:h + 1], in1=ND[:, h, :],
                                                              op0=ALU.mult, op1=ALU.add)
                            empties(v, last, "qC", l, u, p2)
                    step(v.tensor_scalar(dn[:, 0, :], ND[:, :, CD], -1.0, None, ALU.mult))
                    step(v.tensor_tensor(dn[:, 0, :], dn[:, 0, :], ND[:, :, CD], ALU.max))
                    step(v.tensor_tensor(dn[:, 0, :], dn[:, 0, :], se[:, 1, :], ALU.max))
                    step(v.reciprocal(dn[:, 1, :], dn[:, 0, :]))
                    y3 = yC[:, t, :].rearrange("p (h e) -> p h e", h=CH)
                    if C_FIRST[t] == u:
                        step(v.tensor_tensor(y3, ND[:, :, 0:CD], bc(dn[:, 1, :], [P, CH, CD], 2), ALU.mult))
                    else:
                        step(v.tensor_tensor(ND[:, :, 0:CD], ND[:, :, 0:CD], bc(dn[:, 1, :], [P, CH, CD], 2),
                                             ALU.mult))
                        step(v.tensor_tensor(y3, y3, ND[:, :, 0:CD], ALU.add))
                    v.sem_inc(sem("nd_used"), 1)
                    if u in (2, 3):
                        for p2 in range(2):
                            src = wait_filled(v, "kv", l, u, p2)
                            for h in (2 * p2, 2 * p2 + 1):
                                o = 256 * (h % 2)
                                last = v.scalar_tensor_tensor(out=c_state[:, a, h, :], in0=c_state[:, a, h, :],
                                                              scalar=se[:, 2, h:h + 1], in1=src[:, o:o + CD + 1],
                                                              op0=ALU.mult, op1=ALU.add)
                            empties(v, last, "kv", l, u, p2)
                        v.sem_inc(sem("state_ready"), 1)
                    elif u < 2:
                        wait_emptied(v, "kv", l, u, 0)
                        wait_emptied(v, "kv", l, u, 1)
                        if u == 1:
                            v.sem_inc(sem("m_out_ready"), 1)
                    if u + 1 < len(C_UNITS):
                        spread(u + 1)
                    for n, j in C_FILL[2 * u + 1]:
                        merge(n, j)
                for t in range(TILES):
                    y3 = yC[:, t, :].rearrange("p (h e) -> p h e", h=CH)
                    for h in range(CH):
                        last = v.bn_stats(stats[:, h, :], y3[:, h, :])
                    step(last)
                    for h in range(CH):
                        last = v.bn_aggr(aggr[:, h, :], stats[:, h, :])
                    step(last)
                    step(v.tensor_scalar(ms[:, 0:CH], aggr[:, :, 1], EPS, None, ALU.add))
                    inv_sqrt(CH)
                    for h in range(CH):
                        last = v.tensor_scalar(y3[:, h, :], y3[:, h, :], aggr[:, h, 0:1], rs[:, h:h + 1],
                                               ALU.subtract, ALU.mult)
                    step(last)
                    step(v.tensor_tensor(yC[:, t, :], yC[:, t, :], gn, ALU.mult))
                    wait_emptied(v, "proj", l, BLK["co"], t)
                    step(v.tensor_tensor(yC[:, t, :], yC[:, t, :], co[:, t, :], ALU.mult))
                v.sem_inc(sem("yc_ready"), 1)
                for n, j in LAST_MERGES:
                    merge(n, j)
                v.sem_inc(sem("merged_ready"), 1)
                v.wait_ge(sem("gl1_loaded"), 64 * (l + 1))
                for hf in range(2):
                    cols = slice(hf * 512, (hf + 1) * 512)
                    for t in range(TILES):
                        src = wait_filled(v, "out", l, hf, t)
                        empties(v, v.tensor_tensor(z, src, gl1[:, 0 if t == 0 else 1, cols], ALU.mult),
                                "out", l, hf, t)
                        step(v.scalar_tensor_tensor(out=x[:, t, cols], in0=x[:, t, cols], scalar=ALPHA, in1=z,
                                                    op0=ALU.mult, op1=ALU.add))
                        v.sem_inc(sem("x_mixed"), 1)
                for t in range(TILES):
                    layer_norm(x[:, t, :], gl1[:, 2, :], gl1[:, 3, :])
                    v.sem_inc(sem("x_mid"), 1)
                for t in range(TILES):
                    for hf in range(2):
                        modulate(("x2T", l, t, hf), l, t, hf, 2)
                v.wait_ge(sem("state_stored"), 16 * 5 * (l + 1))

                for t in range(TILES):
                    n = n_of(l, t)
                    for i in range(4):
                        wait_emptied(v, "sc", l, t, i)
                    r3 = rep.rearrange("p (b k) -> p b k", b=16)
                    for b in range(16):
                        last = v.max(tops[:, b, 0:8], S[:, b, :])
                    step(last)
                    for b in range(16):
                        v.max_index(ixs_u[:, b, 0:8], tops[:, b, 0:8], S[:, b, :])
                        last = v.match_replace(r3[:, b, :], tops[:, b, 0:8], S[:, b, :], -3.0e38)
                    step(last)
                    v.sem_inc(sem("scores_used"), 1)
                    for b in range(16):
                        last = v.max(tops[:, b, 8:16], r3[:, b, :])
                    step(last)
                    for b in range(16):
                        last = v.max_index(ixs_u[:, b, 8:16], tops[:, b, 8:16], r3[:, b, :])
                    step(last)
                    step(v.tensor_copy(ixs_f, ixs_u))
                    t4 = tops.rearrange("p (h a) k -> p h a k", a=2)
                    c4 = cand.rearrange("p (h a b) -> p h a b", h=PH, a=PTOP)
                    step(v.tensor_tensor(c4, bc(t4[:, :, 0, :], [P, PH, PTOP, PTOP], 3),
                                         bc(t4[:, :, 1, :], [P, PH, PTOP, PTOP], 2), ALU.add))
                    c3 = cand.rearrange("p (h k) -> p h k", h=PH)
                    q3 = rep.rearrange("p (h k) -> p h k", h=PH)
                    for h in range(PH):
                        last = v.max(best[:, h, 0:8], c3[:, h, :])
                    step(last)
                    for h in range(PH):
                        v.max_index(pos[:, h, 0:8], best[:, h, 0:8], c3[:, h, :])
                        last = v.match_replace(q3[:, h, :], best[:, h, 0:8], c3[:, h, :], -3.0e38)
                    step(last)
                    for h in range(PH):
                        last = v.max(best[:, h, 8:16], q3[:, h, :])
                    step(last)
                    for h in range(PH):
                        last = v.max_index(pos[:, h, 8:16], best[:, h, 8:16], q3[:, h, :])
                    step(last)
                    r4 = rep.rearrange("p (h a b) -> p h a b", h=PH, a=PTOP)
                    x4 = ixs_f.rearrange("p (h a) k -> p h a k", a=2)
                    for a, dst in ((0, e_a), (1, e_b)):
                        if a == 0:
                            step(v.tensor_scalar(pos_p, pos, 4, None, ALU.logical_shift_right))
                        else:
                            step(v.tensor_scalar(pos_p, pos, 15, None, ALU.bitwise_and))
                        step(v.tensor_copy(pos_f, pos_p))
                        step(v.tensor_tensor(r4, bc(pos_f, [P, PH, PTOP, PTOP], 3),
                                             iota16.unsqueeze(1).unsqueeze(1).to_broadcast([P, PH, PTOP, PTOP]),
                                             ALU.is_equal))
                        step(v.tensor_tensor(r4, r4, bc(x4[:, :, a, :], [P, PH, PTOP, PTOP], 2), ALU.mult))
                        step(v.tensor_reduce(dst, r4, X, ALU.add))
                    step(v.tensor_scalar(e_a, e_a, float(PKEYS), float(l * EXPERTS), ALU.mult, ALU.add))
                    step(v.tensor_tensor(idx.rearrange("p (h k) -> p h k", h=PH), e_a, e_b, ALU.add))
                    v.sem_inc(sem("idx_ready"), 1)
                    step(v.tensor_copy(gmax, best[:, :, 0]))
                    step(v.tensor_tensor(best, best, bc(gmax, [P, PH, PTOP], 2), ALU.subtract))
                    v.sem_inc(sem("gate_args"), 1)
                    v.wait_ge(sem("gate_exps"), n + 1)
                    step(v.tensor_reduce(gmax, best, X, ALU.add))
                    step(v.reciprocal(gmax, gmax))
                    step(v.tensor_tensor(best, best, bc(gmax, [P, PH, PTOP], 2), ALU.mult))

                    used0 = 2 * PICKS * n
                    if n == 0:
                        v.sem_inc(sem("rows_free"), SLOTS)
                    with v.Fori(0, ROUNDS // 2) as k:
                        for half in range(2):
                            c8 = k * 2 + half
                            for j in range(SLOTS):
                                v.wait_ge(sem(f"row{j}_loaded"), (c8 + (2 * n * ROUNDS + 1)) * 16)
                                v.tensor_tensor_reduce(out=rows[:, j, :], in0=rows[:, j, :], in1=h2[:, t, :],
                                                       scale=1.0, scalar=0.0, op0=ALU.mult, op1=ALU.add,
                                                       accum_out=dots[:, half, j:j + 1])\
                                 .then_inc(sem("rows_free"), 1)
                            v.wait_ge(sem("rows_free"), c8 * SLOTS + (used0 + 2 * SLOTS))
                            v.tensor_copy(act_a[:, bass.ds(c8 * SLOTS, SLOTS)], dots[:, half, :])\
                             .then_inc(sem("dots_kept"), 1)
                            v.wait_ge(sem("dots_kept"), c8 + (n * ROUNDS + 1))
                    v.sem_inc(sem("dots_ready"), 1)
                    step(v.memset(acc, 0.0))
                    v.wait_ge(sem("gelu_ready"), n + 1)
                    step(v.tensor_tensor(coef, act_a, best.rearrange("p h k -> p (h k)"), ALU.mult))
                    with v.Fori(0, ROUNDS // 2) as k:
                        for half in range(2):
                            c8 = k * 2 + half
                            v.tensor_copy(coefs[:, half, :], coef[:, bass.ds(c8 * SLOTS, SLOTS)])\
                             .then_inc(sem("coefs_ready"), 1)
                            v.wait_ge(sem("coefs_ready"), c8 + (n * ROUNDS + 1))
                            for j in range(SLOTS):
                                v.wait_ge(sem(f"row{j}_loaded"), (c8 + (2 * n * ROUNDS + ROUNDS + 1)) * 16)
                                v.scalar_tensor_tensor(out=acc, in0=rows[:, j, :], scalar=coefs[:, half, j:j + 1],
                                                       in1=acc, op0=ALU.mult, op1=ALU.add)\
                                 .then_inc(sem("rows_free"), 1)
                                v.wait_ge(sem("rows_free"), c8 * SLOTS + (used0 + PICKS + SLOTS + j + 1))
                    v.wait_ge(sem("gl2_loaded"), 16 * (4 * l + (3 if t == 0 else 4)))
                    step(v.tensor_tensor(acc, acc, gl2[:, 0, :], ALU.mult))
                    step(v.scalar_tensor_tensor(out=x[:, t, :], in0=x[:, t, :], scalar=ALPHA, in1=acc,
                                                op0=ALU.mult, op1=ALU.add))
                    layer_norm(x[:, t, :], gl2[:, 1, :], gl2[:, 2, :])
                    v.sem_inc(sem("x_final"), 1)
                    if l + 1 < DEPTH and t == 1:
                        modulation(l + 1)

        @block.gpsimd
        def _(g):
            done = [0]

            def powers(count):
                for _ in range(count):
                    done[0] += 1
                    g.wait_ge(sem("squares_ready"), done[0])
                    g.tensor_tensor(rs, ms, nhalf, ALU.pow).then_inc(sem("roots_ready"), 1)

            def store_rows(l):
                for j in range(12):
                    g.wait_ge(sem("mod_row"), 12 * l + j + 1)
                    g.dma_start(mod_dram[l, :, j * 512:(j + 1) * 512], m_stage[:, j % 2, :])\
                     .then_inc(sem(f"mod_stored{j % 2}"), 16)
                g.wait_ge(sem("mod_stored0"), 16 * 6 * (l + 1))
                g.wait_ge(sem("mod_stored1"), 16 * 6 * (l + 1))
                g.sem_inc(sem("mod_stored"), 16 * 12)

            g.memset(ms, 1.0).then_inc(sem("ms_set"), 1)
            g.wait_ge(sem("ms_set"), 1)
            g.wait_ge(sem("consts_loaded"), 16)
            store_rows(0)
            for l in range(DEPTH):
                powers(2 * TILES)
                g.wait_ge(sem("ak_ready"), l + 1)
                wait_emptied(g, "proj", l, BLK["akv"], 0)
                kv = sem("kv_stored")
                g.dma_start(new_a_k[0, l].rearrange("t g d -> t (g d)"), akv[:, 0, 0:128]).then_inc(kv, 16)
                g.dma_start(new_a_v[0, l].rearrange("t g d -> t (g d)"), akv[:, 0, 128:256]).then_inc(kv, 16)
                wait_emptied(g, "proj", l, BLK["dk"], 0)
                wait_emptied(g, "proj", l, BLK["dv"], 0)
                g.dma_start(new_d_k[0, l].rearrange("t h j d -> t (h j d)"), dk[:, 0, :]).then_inc(kv, 16)
                g.dma_start(new_d_v[0, l].rearrange("t h d -> t (h d)"), dv[:, 0, :]).then_inc(kv, 16)
                powers(2 * TILES)
                g.wait_ge(sem("c_new_ready"), 2 * (l + 1))
                g.wait_ge(sem("m_out_ready"), l + 1)
                st = sem("state_stored")
                for a in range(2):
                    g.dma_start(new_c_C[0, l, a].rearrange("h d e -> d h e"), c_new[:, a, :, 0:CD]).then_inc(st, 16)
                with nc.allow_non_contiguous_dma("one column of the states"):
                    for a in range(2):
                        g.dma_start(new_c_n[0, l, a].rearrange("h d -> d h"), c_new[:, a, :, CD]).then_inc(st, 16)
                g.dma_start(new_c_m[0, l].rearrange("a h -> (a h)").unsqueeze(0),
                            m_out[0:1].rearrange("p a h -> p (a h)")).then_inc(st, 16)
                powers(TILES)
                powers(TILES)
                for t in range(TILES):
                    n = n_of(l, t)
                    g.wait_ge(sem("idx_ready"), n + 1)
                    for phase, table in enumerate((peer_u, peer_v)):
                        flat = table.rearrange("l e d -> (l e) d")
                        base = (2 * n + phase) * ROUNDS
                        with g.Fori(0, ROUNDS // 2) as k:
                            for half in range(2):
                                c8 = k * 2 + half
                                g.wait_ge(sem("rows_free"), c8 * SLOTS + (base * SLOTS + 1))
                                g.sem_inc(sem("slots_claimed"), 1)
                                g.tensor_copy(idx_slot[:, half, :], idx[:, bass.ds(c8 * SLOTS, SLOTS)])\
                                 .then_inc(sem("indices_ready"), 1)
                                g.wait_ge(sem("indices_ready"), c8 + (base + 1))
                                g.sem_inc(sem("slots_claimed"), 1)
                                for j in range(SLOTS):
                                    g.wait_ge(sem("rows_free"), c8 * SLOTS + (base * SLOTS + j + 1))
                                    g.sem_inc(sem("slots_claimed"), 1)
                                    g.indirect_dma_start(rows[:, j, :], None, flat,
                                                         bass.IndirectOffsetOnAxis(ap=idx_slot[:, half, j:j + 1], axis=0))\
                                     .then_inc(sem(f"row{j}_loaded"), 16)
                    powers(1)
                    if l + 1 < DEPTH and t == 1:
                        store_rows(l + 1)
            g.wait_ge(sem("kv_stored"), 64 * DEPTH)
            g.wait_ge(sem("state_stored"), 16 * 5 * DEPTH)


_INS = ["x_prompt", "x_sample", "cache_a_k", "cache_a_v", "cache_d_k", "cache_d_v", "state_c_C", "state_c_n",
        "state_c_m", "c", "c_ctx", "w_mod", "b_mod", "w_in", "attn_qk_gain", "gmlp_ws", "gmlp_b",
        "mlstm_gate_bias", "mlstm_gn", "diff_lambda", "diff_gn", "w_branch", "w_out", "ln_g", "ln_b",
        "peer_wq", "peer_keys", "peer_u", "peer_v"]
_OUTS = [(1, P, DM), (1, 2 * P, DM), (1, DEPTH, P, AG, AD), (1, DEPTH, P, AG, AD), (1, DEPTH, P, DH, 2, DD),
         (1, DEPTH, P, DH, DV), (1, DEPTH, 2, CH, CD, CD), (1, DEPTH, 2, CH, CD), (1, DEPTH, 2, CH)]


def constants(np):
    out = np.zeros((P, 1056), np.float32)
    s, t = np.arange(P)[:, None], np.arange(P)[None, :]
    out[:, 0:128] = s == t
    out[:, 128:256] = 1.0
    out[:, 256:384] = s <= t
    out[:, 384:512] = s >= t
    out[:, 512:640] = np.where(t <= s, 0.0, NEG)
    out[:, 640:768] = np.where(t >= s, 0.0, NEG)
    quarter = AD // 4
    inv = np.float32(10000.0) ** (-np.arange(quarter, dtype=np.float32) / np.float32(quarter))
    cos, sin = np.zeros((2 * P, 2, 2, quarter)), np.zeros((2 * P, 2, 2, quarter))
    token = np.arange(2 * P)
    for a, at in enumerate((token // GW, token % GW)):
        ang = (at[:, None].astype(np.float32) * inv[None, :]).astype(np.float32).astype(np.float64)
        cos[:, a, 0], cos[:, a, 1] = np.cos(ang), np.cos(ang)
        sin[:, a, 0], sin[:, a, 1] = -np.sin(ang), np.sin(ang)
    tables = np.stack([cos.reshape(2, P, AD), sin.reshape(2, P, AD)])
    out[:, 768:1024] = tables.transpose(2, 0, 1, 3).reshape(P, 256)
    out[:, 1024:1040] = np.arange(16)
    out[:, 1040:1056] = -0.5
    return out


def kernel(**inputs):
    import numpy as np
    import concourse.bacc as bacc
    from concourse.bass_utils import run_bass_kernel_spmd

    nc = bacc.Bacc("TRN2", target_bir_lowering=False, num_devices=1)
    arrays, args = {}, []
    for name in _INS:
        a = np.ascontiguousarray(inputs[name])
        arrays[f"in_{name}"] = a
        args.append(nc.dram_tensor(f"in_{name}", a.shape, mybir.dt.float32, kind="ExternalInput").ap())
    arrays["in_consts"] = constants(np)
    args.append(nc.dram_tensor("in_consts", (P, 1056), mybir.dt.float32, kind="ExternalInput").ap())
    for i, shape in enumerate(_OUTS):
        args.append(nc.dram_tensor(f"out_{i}", shape, mybir.dt.float32, kind="ExternalOutput").ap())
    build(nc, *args)
    r = run_bass_kernel_spmd(nc, [arrays], core_ids=[0])
    return tuple(np.asarray(r.results[0][f"out_{i}"]) for i in range(len(_OUTS)))
```

```python
import math
from contextlib import ExitStack

import concourse.bass as bass
from concourse import mybir

DM = 1024
DEPTH = 2
P = 128
TILES = 3
T = TILES * P
KC = DM // P
BW = DM // 2
AH, AG, AD = 8, 2, 64
CH, CD = 4, 128
DH, DD, DV = 4, 64, 128
BG = 4
NB = 4
GW = 64
PH, PKEYS, PTOP, PQ = 8, 128, 16, 128
EXPERTS = PKEYS * PKEYS
PICKS = PH * PTOP
EPS = 1e-6
ALPHA = (2 * DEPTH) ** 0.25
NEG = -1.0e30

C_AQ, C_AK, C_BU, C_BV, C_CQ, C_CK, C_CV, C_CO, C_CG, C_DQ, C_DK, C_DVV = (
    0, 512, 768, 1280, 1792, 2304, 2816, 3328, 3840, 3856, 4368, 4880)
C_GATES = 5392
BLOCKS = [("aq", C_AQ, 512), ("akv", C_AK, 256), ("dq", C_DQ, 512), ("dk", C_DK, 512),
          ("dv", C_DVV, 512), ("cg", C_CG, 16), ("cq", C_CQ, 512), ("ck", C_CK, 512),
          ("cv", C_CV, 512), ("bv", C_BV, 512), ("bu", C_BU, 512), ("co", C_CO, 512)]
BLK = {name: i for i, (name, _, _) in enumerate(BLOCKS)}

KEY_SLOT_OF_TILE = {1: 0, 2: 1, 3: 2, 0: 3}
TILE_OF_KEY_SLOT = [1, 2, 3, 0]
KEY_SLOTS = {0: [3], 1: [0, 1, 2], 2: [0, 1, 2]}

C_UNITS = [(0, 0), (0, 1), (1, 0), (2, 1), (2, 0), (1, 1)]
C_FIRST = {0: 0, 1: 2, 2: 3}
C_UPDATES = (0, 1, 2, 3)

A_UNITS = [(t, h) for t in range(TILES) for h in range(AH)]
D_UNITS = [(t, h) for t in range(TILES) for h in range(DH)]
LAG_T, LAG_V = 2, 3

FIRST_BLOCKS = 4
_REST = [(b, t) for b in range(FIRST_BLOCKS, len(BLOCKS)) for t in range(TILES)]
A_FILL = {2 * k: _REST[k] for k in range(14)}
D_FILL = {2 * k + 1: _REST[14 + k] for k in range(7)}
LAST_FILL = _REST[21:]

MERGE_ORDER = (0, 3, 1, 2)
MERGES = [(n, j) for n in MERGE_ORDER for j in range(KC)]
NORM_MERGES = MERGES[(NB - 1) * KC - TILES:(NB - 1) * KC]
LAST_MERGES = MERGES[(NB - 1) * KC:]
STEP_MERGES = MERGES[:(NB - 1) * KC - TILES]
GAPS = 2 * len(C_UNITS)
C_FILL = [STEP_MERGES[2 * g:2 * g + 2] for g in range(GAPS)]
assert [n for n, _ in LAST_MERGES] == [2] * KC

SLOTS = 8
ROUNDS = PICKS // SLOTS


MODS = 12
Q_ORDER = (0, 2, 3, 1)
Q_HEADS = [4 * c + k for c in Q_ORDER for k in range(4)]
GATE_AT = 12
PE_ROUNDS = 4
PE_PICKS = PE_ROUNDS * SLOTS


def mod_jobs(l):
    out = []
    for j in range(MODS):
        out.append(("mod", l, j))
        if j // 2 in (0, 1, 3, 4):
            out.append(("mcol", l, j))
    return out


def tensor_jobs():
    out = mod_jobs(0)
    for l in range(DEPTH):
        out += [("xT", l, t, hf) for t in range(TILES) for hf in range(2)]
        out += [("proj", l, b, t) for b in range(FIRST_BLOCKS) for t in range(TILES)]
        out += [("wsT", l)]
        out += [("qTA", l, t) for t in range(TILES)] + [("kTA", l, s) for s in range(4)]
        for i in range(len(A_UNITS) + LAG_V):
            if i < len(A_UNITS):
                out.append(("sA", l, i))
            if 0 <= i - LAG_T < len(A_UNITS):
                out.append(("pTA", l, i - LAG_T))
            if i >= LAG_V and (i - LAG_V) % AH == 0:
                out.append(("oA", l, (i - LAG_V) // AH))
            if i in A_FILL:
                out.append(("proj", l, *A_FILL[i]))
        out += [("qTD", l, t) for t in range(TILES)] + [("kTD", l, s) for s in range(4)]
        for i in range(len(D_UNITS) + LAG_V):
            if i < len(D_UNITS):
                out += [("sD", l, i, 0), ("sD", l, i, 1)]
            if 0 <= i - LAG_T < len(D_UNITS):
                out.append(("pTD", l, i - LAG_T))
            if i >= LAG_V and (i - LAG_V) % DH == 0:
                out.append(("oD", l, (i - LAG_V) // DH))
            if i in D_FILL:
                out.append(("proj", l, *D_FILL[i]))
        out += [("bmm", l, t) for t in range(TILES)]
        out += [("qTC", l, t) for t in range(TILES)] + [("kTC", l, t) for t in range(TILES)]
        out += [("sC", l, t) for t in range(TILES)]
        out += [("yT", l, n, t) for n in (0, 1) for t in range(TILES)]
        out += [("proj", l, b, t) for b, t in LAST_FILL]
        out += [("cum", l)]
        out += [("yT", l, 3, t) for t in range(TILES)]
        for u, (t, d) in enumerate(C_UNITS):
            out += [("rb", l, u)]
            for n, j in C_FILL[2 * u]:
                out += [("gate", l, n, j), ("br", l, n, j)]
            out += [("wT", l, u)]
            if u in C_UPDATES:
                out += [("kv", l, u, 0), ("kv", l, u, 1)]
            out += [("num", l, u, 0), ("num", l, u, 1)]
            if t:
                out += [("qC", l, u, 0), ("qC", l, u, 1)]
            for n, j in C_FILL[2 * u + 1]:
                out += [("gate", l, n, j), ("br", l, n, j)]
        for n, j in NORM_MERGES:
            out += [("gate", l, n, j), ("br", l, n, j)]
        out += [("yT", l, 2, t) for t in range(TILES)]
        out += [("kT", l, i) for i in range(4)]
        for n, j in LAST_MERGES:
            out += [("gate", l, n, j), ("br", l, n, j)]
        out += [("out", l, hf, t) for t in (0, 1) for hf in range(2)]
        out += [("x2T", l, 0, hf) for hf in range(2)] + [("h2", l, 0, hf) for hf in range(2)]
        out += [("out", l, hf, 2) for hf in range(2)]
        out += [("x2T", l, 1, hf) for hf in range(2)]
        out += [("q0", l, c) for c in Q_ORDER[:2]]
        out += [("x2T", l, 2, hf) for hf in range(2)]
        out += [("sc", l, 0, c) for c in Q_ORDER[:2]]
        out += [("q0", l, Q_ORDER[2]), ("h2", l, 1, 0), ("h2", l, 1, 1), ("sc", l, 0, Q_ORDER[2])]
        out += [("q0", l, Q_ORDER[3]), ("h2", l, 2, 0), ("h2", l, 2, 1), ("sc", l, 0, Q_ORDER[3])]
        out += [("q", l, j) for j in Q_HEADS]
        out += [("sc", l, 1, i) for i in range(4)]
        if l + 1 < DEPTH:
            out += mod_jobs(l + 1)
        out += [("sc", l, 2, i) for i in range(4)]
        out += [("vsum", l, t, hf) for t in range(TILES - 1) for hf in range(2)]
    return out


WIDE = {"xT", "bmm", "qTC", "kTC", "sC", "yT", "cum", "rb", "gate", "br", "wT", "kv", "num", "qC", "kT", "out", "x2T",
        "h2", "q0", "q"}
HELD = {"oA": (6, 7), "oD": (6, 7), "vsum": (6, 7)}
BANKS = 6


def turns(jobs):
    used, fills, out, i, held = [0] * 8, [0] * 8, {}, 0, 0
    for j in jobs:
        if j[0] in HELD:
            b = HELD[j[0]][held % 2]
            held += 1
        else:
            b = i % (8 if j[0] in WIDE else BANKS)
            i = b + 1
        out[j] = (b, used[b], fills[b])
        used[b] += 1
        if j[0] not in HELD:
            fills[b] += 1
    return out


N_PARAMS = 16
RING = 3
SLOT_W = KC * 512


def weight_loads():
    out = [(("mod", 0, j), ("mod", 0, j)) for j in range(MODS)]
    for l in range(DEPTH):
        out += [(("proj", l, b), ("proj", l, b, TILES - 1)) for b in range(len(BLOCKS))]
        for n in MERGE_ORDER:
            if n == MERGE_ORDER[-1]:
                out += [(("keys", l), ("kT", l, 3))]
            out += [(("wg", l, n, 0), ("gate", l, n, 3)), (("wb", l, n), ("br", l, n, 7)),
                    (("wg", l, n, 1), ("gate", l, n, 7))]
        out += [(("out", l, hf), ("out", l, hf, TILES - 1)) for hf in range(2)]
        out += [(("q", l, c), ("q", l, 4 * c + 3)) for c in (Q_ORDER[0], Q_ORDER[3])]
        if l + 1 < DEPTH:
            out += [(("mod", l + 1, j), ("mod", l + 1, j)) for j in range(MODS)]
    return out


def build(nc, x_prompt, x_sample, cache_a_k, cache_a_v, cache_d_k, cache_d_v, state_c_C, state_c_n,
          state_c_m, c, c_ctx, w_mod, b_mod, w_in, attn_qk_gain, gmlp_ws, gmlp_b, mlstm_gate_bias,
          mlstm_gn, diff_lambda, diff_gn, w_branch, w_out, ln_g, ln_b, peer_wq, peer_keys, peer_u,
          peer_v, consts, y_prompt, y_sample, new_a_k, new_a_v, new_d_k, new_d_v, new_c_C, new_c_n,
          new_c_m):
    f32, u32 = mybir.dt.float32, mybir.dt.uint32
    ALU, ACT, X = mybir.AluOpType, mybir.ActivationFunctionType, mybir.AxisListType.X
    ctx = ExitStack()
    with ctx:
        def sb(name, width, dt=f32, parts=P):
            return ctx.enter_context(nc.sbuf_tensor(name, [parts, width], dt))[:, :]

        named = {}

        def sem(name):
            if name not in named:
                named[name] = ctx.enter_context(nc.semaphore(name))
            return named[name]

        x = sb("x", TILES * DM).rearrange("p (t d) -> p t d", t=TILES)
        hT = sb("hT", KC * T).rearrange("p (c t) -> p c t", c=KC)
        ring = sb("ring", RING * SLOT_W).rearrange("p (s n) -> p s n", s=RING)
        work = sb("work", 3076)
        cst = sb("cst", 1024 + 32)
        pars = sb("pars", 1180)
        states = sb("states", 2 * 2 * CH * (CD + 1))
        small = sb("small", 512)
        ARENA = 26684
        arena = sb("arena", ARENA)
        top = [0]

        def take(width):
            at = top[0]
            top[0] += width
            assert top[0] <= ARENA, top[0]
            return arena[:, at:at + width]

        def tiled(width, n=TILES):
            return take(width * n).rearrange("p (t d) -> p t d", t=n)

        aq, akv, bu, bv = tiled(512), tiled(256, 4), tiled(512), tiled(512)
        cq, ck = tiled(512), tiled(512)
        cv = tiled(CH * (CD + 1)).rearrange("p t (h e) -> p t h e", h=CH)
        co, cg, dq = tiled(512), tiled(16), tiled(512)
        d_at = top[0]
        dk, dv = tiled(512, 4), tiled(512, 4)
        qTA, kTA = take(4 * T).rearrange("p (b t) -> p b t", b=4), take(2 * 512).rearrange("p (g k) -> p g k", g=2)
        qTD, kTD = take(4 * T).rearrange("p (b t) -> p b t", b=4), take(4 * 512).rearrange("p (g k) -> p g k", g=4)
        q_at = top[0]
        qTC, kTC = take(4 * T).rearrange("p (b t) -> p b t", b=4), take(4 * T).rearrange("p (b t) -> p b t", b=4)
        wsT = arena[:, q_at + 512:q_at + 1024].rearrange("p (g q) -> p g q", g=BG)
        ws_raw = arena[:, q_at:q_at + 512].rearrange("p (g q) -> p g q", g=BG)
        k_dup = arena[:, q_at + 4 * T:q_at + 4 * T + 1024].rearrange("p (s g n) -> p s g n", s=4, g=AG)
        sC = cq
        merged = arena[:, d_at:d_at + KC * T].rearrange("p (c t) -> p c t", c=KC)
        yA, yB, yC, yD = aq, bv, dq, dk[:, 0:TILES, :]
        ys = [yA, yB, yC, yD]
        yT = [qTA, bu.rearrange("p t d -> p (t d)").rearrange("p (b t) -> p b t", b=4), qTC, qTD]
        top[0] = 0
        h2 = tiled(DM)
        qTp = take(16 * T).rearrange("p (b t) -> p b t", b=16)
        keysT = take(16 * P).rearrange("p (b k) -> p b k", b=16)
        S = take(16 * PKEYS).rearrange("p (b k) -> p b k", b=16)
        cand = take(2048)
        rep = take(2048)
        rows = take(SLOTS * DM).rearrange("p (s d) -> p s d", s=SLOTS)
        acc = take(DM)
        q_extra = rows.rearrange("p s d -> p (s d)").rearrange("p (a n) -> p a n", a=2)
        ln1 = [h2[:, 2, :], acc]
        spread_w = qTp.rearrange("p b t -> p (b t)")[:, 0:PE_PICKS * P].rearrange("p (k q) -> p k q", k=PE_PICKS)
        gl2 = hT.rearrange("p c t -> p (c t)").rearrange("p (a d) -> p a d", a=3)

        pr = work[:, 0:6 * 384].rearrange("p (s k) -> p s k", s=6)
        pt = work[:, 6 * 384:8 * 384].rearrange("p (s k) -> p s k", s=2)
        diag = work[:, 0:512].rearrange("p (h s) -> p h s", h=CH)
        kws = diag
        Mx = work[:, 512:1024].rearrange("p (h s) -> p h s", h=CH)
        Wc = work[:, 1024:1536].rearrange("p (h s) -> p h s", h=CH)
        WT = work[:, 1536:2048].rearrange("p (h s) -> p h s", h=CH)
        ND = work[:, 2048:2048 + CH * (CD + 1)].rearrange("p (h e) -> p h e", h=CH)
        tmp = work[:, 2564:2564 + 512]
        kd_flat = kTD.rearrange("p g k -> p (g k)")
        sg = kd_flat[:, 0:2 * T].rearrange("p (s k) -> p s k", s=2)
        prod = kd_flat[:, 2 * T:3 * T]
        z = work[:, 0:512]
        gates1 = work[:, 512:512 + 2 * DM].rearrange("p (a d) -> p a d", a=2)
        m_stage = work[0:2, 0:1024].rearrange("p (s n) -> p s n", s=2)
        b_stage = work[0:1, 1024:2048].rearrange("p (s n) -> p s n", s=2)

        ident, ones = cst[:, 0:128], cst[:, 128:256]
        tri = cst[:, 256:512].rearrange("p (a t) -> p a t", a=2)
        negmask = cst[:, 512:768].rearrange("p (a t) -> p a t", a=2)
        rope_cs = cst[:, 768:1024].rearrange("p (a t d) -> p a t d", a=2, t=2)
        iota16 = cst[:, 1024:1040]
        nhalf = cst[:, 1040:1056]

        gains = pars[:, 0:128].rearrange("p (a d) -> p a d", a=2)
        cg_bias = pars[:, 128:144]
        b_bias = pars[:, 144:148]
        lam_v = kTD[:, 0, 0:256].rearrange("p (a b d) -> p a b d", a=2, b=2)
        gn = pars[:, 148:660]
        dgn = pars[:, 660:1172]
        neg_lam = pars[:, 1172:1173]
        lam_e = pars[:, 1174:1176]

        SW = CH * (CD + 1)
        c_state = states[:, 0:2 * SW].rearrange("p (a h e) -> p a h e", a=2, h=CH)
        c_new = states[:, 2 * SW:4 * SW].rearrange("p (a h e) -> p a h e", a=2, h=CH)

        modcol = small[:, 0:128].rearrange("p (l a c n) -> p l a c n", l=DEPTH, a=4, c=KC)
        silu_c = small[:, 128:144].rearrange("p (c n) -> p c n", c=KC)
        sig_c = small[:, 144:160].rearrange("p (c n) -> p c n", c=KC)
        negm = small[:, 160:184]
        sums = small[:, 184:208]
        rsum = small[:, 208:232]
        ms = small[:, 232:248]
        rs = small[:, 248:264]
        stats = small[:, 264:264 + 24].rearrange("p (a s) -> p a s", a=4)
        aggr = small[:, 288:296].rearrange("p (a s) -> p a s", a=4)
        m_lat = small[:, 296:304].rearrange("p (a h) -> p a h", a=2)
        m_out = small[:, 304:312].rearrange("p (a h) -> p a h", a=2)
        lf = small[:, 312:336].rearrange("p (a t h) -> p a t h", a=2, t=TILES)
        lt = small[:, 336:360].rearrange("p (a t h) -> p a t h", a=2, t=TILES)
        csum = small[:, 360:408].rearrange("p (k a t h) -> p k a t h", k=2, a=2, t=TILES)
        rr = small[:, 408:432].rearrange("p (a t h) -> p a t h", a=2, t=TILES)
        mxr, mxl, mra = small[:, 432:436], small[:, 436:440], small[:, 440:444]
        se = small[:, 444:460].rearrange("p (k h) -> p k h", k=4)
        dn = small[:, 460:468].rearrange("p (k h) -> p k h", k=2)
        zero4 = small[:, 468:472]
        idx_slot = sb("idx_slot", 2 * SLOTS, u32).rearrange("p (a s) -> p a s", a=2)
        dots = small[:, 472:488].rearrange("p (a s) -> p a s", a=2)
        coefs = small[:, 488:504].rearrange("p (a s) -> p a s", a=2)
        gmax = small[:, 504:512]
        cond_raw = sig_c

        tops = states[:, 0:256].rearrange("p (b k) -> p b k", b=16)
        ixs_u = states[:, 256:512].bitcast(u32).rearrange("p (b k) -> p b k", b=16)
        ixs_f = states[:, 512:768].rearrange("p (b k) -> p b k", b=16)
        best = states[:, 768:896].rearrange("p (h k) -> p h k", h=PH)
        pos = states[:, 896:1024].bitcast(u32).rearrange("p (h k) -> p h k", h=PH)
        pos_p = states[:, 1024:1152].bitcast(u32).rearrange("p (h k) -> p h k", h=PH)
        pos_f = states[:, 1152:1280].rearrange("p (h k) -> p h k", h=PH)
        e_a = states[:, 1280:1408].rearrange("p (h k) -> p h k", h=PH)
        e_b = states[:, 1408:1536].rearrange("p (h k) -> p h k", h=PH)
        idx = states[:, 1536:1792].bitcast(u32).rearrange("p (a k) -> p a k", a=2)
        act_a = states[:, 1792:1920]
        coef = states[:, 1920:2048]

        bank = [ctx.enter_context(nc.psum_tensor(f"bank{i}", [P, 512], f32))[:, :] for i in range(8)]
        mod_dram = nc.dram_tensor("mod_rows", (DEPTH, 2, 6 * DM), f32, kind="Internal").ap()

        jobs = tensor_jobs()
        turn = turns(jobs)
        filled = [sem(f"bank{i}_filled") for i in range(8)]
        emptied = [sem(f"bank{i}_emptied") for i in range(8)]
        loads = weight_loads()
        load_at = {key: i for i, (key, _) in enumerate(loads)}
        slot_loaded = [sem(f"weights{i}_loaded") for i in range(RING)]

        def wait_filled(eng, *job):
            b, _, k = turn[job]
            eng.wait_ge(filled[b], k + 1)
            return bank[b]

        def wait_emptied(eng, *job):
            b, k, _ = turn[job]
            eng.wait_ge(emptied[b], k + 1)

        def empties(eng, ins, *job):
            b, k, _ = turn[job]
            ins.then_inc(emptied[b], 1)
            eng.wait_ge(emptied[b], k + 1)

        def slot(eng, *key):
            i = load_at[key]
            if eng is not None:
                eng.wait_ge(slot_loaded[i % RING], 16 * (i // RING + 1))
            return ring[:, i % RING, :]

        def n_of(l, t):
            return l * TILES + t

        block = ctx.enter_context(nc.Block())

        @block.sync
        def _(sp):
            sp.dma_start(cst, consts).then_inc(sem("consts_loaded"), 16)
            sp.dma_start(x[:, 0, :], x_prompt[0]).then_inc(sem("x_loaded"), 16)
            sp.dma_start(x[:, 1:3, :], x_sample[0].rearrange("(t p) d -> p t d", p=P)).then_inc(sem("x_loaded"), 16)

            def load(key):
                i = load_at[key]
                if i >= RING:
                    wait_filled(sp, *loads[i - RING][1])
                dst = ring[:, i % RING, :]
                kind, l = key[0], key[1]
                if kind == "mod":
                    j = key[2]
                    if j >= 2 or l:
                        wait_filled(sp, "mod", *((l, j - 2) if j >= 2 else (l - 1, MODS - 2 + j)))
                    if l and j == 0:
                        sp.wait_ge(sem("x_mixed"), 2 * TILES * l)
                    sp.dma_start(b_stage[:, j % 2, :], b_mod[l, j * 512:(j + 1) * 512].unsqueeze(0))\
                      .then_inc(sem(f"b_mod{j % 2}_loaded"), 16)
                    src = w_mod[l, :, j * 512:(j + 1) * 512]
                elif kind == "proj":
                    _, s, w = BLOCKS[key[2]]
                    sp.dma_start(dst[:, 0:KC * w].rearrange("p (c n) -> p c n", c=KC),
                                 w_in[l, :, s:s + w].rearrange("(c p) n -> p c n", p=P))\
                      .then_inc(slot_loaded[i % RING], 16)
                    return
                elif kind == "wg":
                    s = C_GATES + key[2] * DM + key[3] * 512
                    src = w_in[l, :, s:s + 512]
                elif kind == "wb":
                    sp.dma_start(dst.rearrange("p (c n) -> p c n", c=4),
                                 w_branch[l, key[2]].rearrange("(c p) n -> p c n", p=P))\
                      .then_inc(slot_loaded[i % RING], 16)
                    return
                elif kind == "out":
                    src = w_out[l, :, key[2] * 512:(key[2] + 1) * 512]
                elif kind == "q":
                    src = peer_wq[l, :, key[2] * 512:(key[2] + 1) * 512]
                else:
                    sp.dma_start(dst[:, 0:16 * PQ].rearrange("p (b d) -> p b d", b=16),
                                 peer_keys[l].rearrange("h a k d -> k (h a) d")).then_inc(slot_loaded[i % RING], 16)
                    return
                sp.dma_start(dst.rearrange("p (c n) -> p c n", c=KC), src.rearrange("(c p) n -> p c n", p=P))\
                  .then_inc(slot_loaded[i % RING], 16)

            with nc.allow_non_contiguous_dma("columns of small vectors"):
                sp.dma_start(cond_raw[:, :, 0], c_ctx.rearrange("(c p) -> p c", p=P)).then_inc(sem("cond_loaded"), 16)
                sp.dma_start(cond_raw[:, :, 1], c[0].rearrange("(c p) -> p c", p=P)).then_inc(sem("cond_loaded"), 16)
            for j in range(MODS):
                load(("mod", 0, j))
            for l in range(DEPTH):
                for b in range(RING):
                    load(("proj", l, b))
                if l:
                    sp.wait_ge(sem("x_final"), n_of(l - 1, TILES - 1) + 1)
                pl = sem("params_loaded")
                sp.dma_start(gains, attn_qk_gain[l].rearrange("a d -> (a d)").partition_broadcast(P)).then_inc(pl, 16)
                sp.dma_start(cg_bias, mlstm_gate_bias[l].rearrange("a b h -> (a b h)").partition_broadcast(P)).then_inc(pl, 16)
                sp.dma_start(lam_v, diff_lambda[l].rearrange("a d -> (a d)").partition_broadcast(P)
                             .rearrange("p (a b d) -> p a b d", a=2, b=2)).then_inc(pl, 16)
                sp.dma_start(gn, mlstm_gn[l].rearrange("h d -> (h d)").partition_broadcast(P)).then_inc(pl, 16)
                sp.dma_start(dgn, diff_gn[l].rearrange("h d -> (h d)").partition_broadcast(P)).then_inc(pl, 16)
                with nc.allow_non_contiguous_dma("columns of small vectors"):
                    sp.dma_start(b_bias, gmlp_b[l].rearrange("g p -> p g")).then_inc(pl, 16)
                    for a in range(2):
                        sp.dma_start(c_state[:, a, :, CD], state_c_n[0, l, a].rearrange("h d -> d h")).then_inc(pl, 16)
                sp.dma_start(ws_raw, gmlp_ws[l].rearrange("g p q -> p g q")).then_inc(pl, 16)
                sp.dma_start(m_lat.rearrange("p a h -> p (a h)"),
                             state_c_m[0, l].rearrange("a h -> (a h)").partition_broadcast(P)).then_inc(pl, 16)
                sp.dma_start(akv[:, 3, 0:128], cache_a_k[0, l].rearrange("t g d -> t (g d)")).then_inc(pl, 16)
                sp.dma_start(akv[:, 3, 128:256], cache_a_v[0, l].rearrange("t g d -> t (g d)")).then_inc(pl, 16)
                sp.dma_start(dk[:, 3, :], cache_d_k[0, l].rearrange("t h j d -> t (h j d)")).then_inc(pl, 16)
                sp.dma_start(dv[:, 3, :], cache_d_v[0, l].rearrange("t h d -> t (h d)")).then_inc(pl, 16)
                for a in range(2):
                    sp.dma_start(c_state[:, a, :, 0:CD], state_c_C[0, l, a].rearrange("h d e -> d h e")).then_inc(pl, 16)
                for b in range(RING, len(BLOCKS)):
                    load(("proj", l, b))
                for n in MERGE_ORDER:
                    if n == MERGE_ORDER[-1]:
                        load(("keys", l))
                    load(("wg", l, n, 0))
                    load(("wb", l, n))
                    load(("wg", l, n, 1))
                wait_filled(sp, "yT", l, 2, TILES - 1)
                for i in range(2):
                    sp.wait_ge(sem(f"mod_stored{i}"), 16 * MODS // 2 * (l + 1))
                g1 = sem("gl1_loaded")
                for n in range(2):
                    sp.dma_start(gates1[:, n, :], mod_dram[l, n, 2 * DM:3 * DM].partition_broadcast(P)).then_inc(g1, 16)
                sp.dma_start(ln1[0], ln_g[l, 0].partition_broadcast(P)).then_inc(g1, 16)
                sp.dma_start(ln1[1], ln_b[l, 0].partition_broadcast(P)).then_inc(g1, 16)
                for hf in range(2):
                    load(("out", l, hf))
                load(("q", l, Q_ORDER[0]))
                sp.wait_ge(sem("merged_ready"), l + 1)
                for i in range(2):
                    k = Q_ORDER[1 + i]
                    sp.dma_start(q_extra[:, i, :].rearrange("p (c n) -> p c n", c=KC),
                                 peer_wq[l, :, k * 512:(k + 1) * 512].rearrange("(c p) n -> p c n", p=P))\
                      .then_inc(sem(f"q_extra{i}_loaded"), 16)
                load(("q", l, Q_ORDER[3]))
                if l + 1 < DEPTH:
                    for j in range(RING):
                        load(("mod", l + 1, j))
                wait_filled(sp, "q", l, Q_HEADS[-1])
                wait_filled(sp, "h2", l, TILES - 1, 1)
                g2 = sem("gl2_loaded")
                sp.dma_start(gl2[:, 0, :], mod_dram[l, 0, 5 * DM:6 * DM].partition_broadcast(P)).then_inc(g2, 16)
                sp.dma_start(gl2[:, 1, :], ln_g[l, 1].partition_broadcast(P)).then_inc(g2, 16)
                sp.dma_start(gl2[:, 2, :], ln_b[l, 1].partition_broadcast(P)).then_inc(g2, 16)
                if l + 1 < DEPTH:
                    for j in range(RING, MODS):
                        load(("mod", l + 1, j))
                sp.wait_ge(sem("x_final"), n_of(l, 0) + 1)
                sp.dma_start(gl2[:, 0, :], mod_dram[l, 1, 5 * DM:6 * DM].partition_broadcast(P)).then_inc(g2, 16)
            sp.wait_ge(sem("x_final"), n_of(DEPTH - 1, 0) + 1)
            sp.dma_start(y_prompt[0], x[:, 0, :]).then_inc(sem("y_stored"), 16)
            for t in (1, 2):
                sp.wait_ge(sem("x_final"), n_of(DEPTH - 1, t) + 1)
                sp.dma_start(y_sample[0, (t - 1) * P:t * P, :], x[:, t, :]).then_inc(sem("y_stored"), 16)
            sp.wait_ge(sem("y_stored"), 48)

        @block.tensor
        def _(pe):
            at = [0]

            def begin(*job):
                assert jobs[at[0]] == job, (jobs[at[0]], job)
                at[0] += 1
                b, k, _ = turn[job]
                if k:
                    pe.wait_ge(emptied[b], k)
                return bank[b]

            def done(ins, *job):
                ins.then_inc(filled[turn[job][0]], 1)

            def transposes(job, srcs):
                out = begin(*job)
                for i, s in enumerate(srcs):
                    last = pe.transpose(out[:, i * P:(i + 1) * P], s, ident)
                done(last, *job)

            def modulation(l):
                for j in range(MODS):
                    out = begin("mod", l, j)
                    pe.wait_ge(sem(f"b_mod{j % 2}_loaded"), 16 * (MODS // 2 * l + j // 2 + 1))
                    pe.matmul(out[0:2, :], ones[0:1, 0:2], b_stage[:, j % 2, :], start=True, stop=False)
                    w = slot(pe, "mod", l, j).rearrange("p (c n) -> p c n", c=KC)
                    for k in range(KC):
                        last = pe.matmul(out[0:2, :], silu_c[:, k, :], w[:, k, :], start=False, stop=k == KC - 1)
                    done(last, "mod", l, j)
                    if j // 2 in (0, 1, 3, 4):
                        out = begin("mcol", l, j)
                        wait_emptied(pe, "mod", l, j)
                        for i in range(4):
                            last = pe.matmul(out[:, 2 * i:2 * i + 2], m_stage[:, j % 2, i * P:(i + 1) * P],
                                             ident[0:2, 0:2], start=True, stop=True)
                        done(last, "mcol", l, j)

            pe.wait_ge(sem("consts_loaded"), 16)
            pe.wait_ge(sem("silu_ready"), 1)
            modulation(0)
            for l in range(DEPTH):
                if l == 0:
                    pe.wait_ge(sem("x_loaded"), 32)
                for t in range(TILES):
                    if l:
                        pe.wait_ge(sem("x_final"), n_of(l - 1, t) + 1)
                    for hf in range(2):
                        transposes(("xT", l, t, hf), [x[:, t, (4 * hf + i) * P:(4 * hf + i + 1) * P] for i in range(4)])
                def project(b, t):
                    w = BLOCKS[b][2]
                    wt = slot(pe, "proj", l, b)[:, 0:KC * w].rearrange("p (c n) -> p c n", c=KC)
                    if b == 0:
                        wait_emptied(pe, "xT", l, t, 1)
                    out = begin("proj", l, b, t)
                    for k in range(KC):
                        last = pe.matmul(out[:, 0:w], hT[:, k, t * P:(t + 1) * P], wt[:, k, :],
                                         start=k == 0, stop=k == KC - 1)
                    done(last, "proj", l, b, t)

                def merge(n, j):
                    if j == 0:
                        for t in range(TILES):
                            wait_emptied(pe, "yT", l, n, t)
                    wg = slot(pe, "wg", l, n, j // 4).rearrange("p (c n) -> p c n", c=KC)
                    out = begin("gate", l, n, j)
                    for k in range(KC):
                        last = pe.matmul(out[:, 0:T], wg[:, k, (j % 4) * P:(j % 4 + 1) * P], hT[:, k, :],
                                         start=k == 0, stop=k == KC - 1)
                    done(last, "gate", l, n, j)
                    wb = slot(pe, "wb", l, n).rearrange("p (c n) -> p c n", c=4)
                    out = begin("br", l, n, j)
                    for k in range(4):
                        last = pe.matmul(out[:, 0:T], wb[:, k, j * P:(j + 1) * P], yT[n][:, k, :],
                                         start=k == 0, stop=k == 3)
                    done(last, "br", l, n, j)

                def y_transposed(n):
                    for t in range(TILES):
                        transposes(("yT", l, n, t), [ys[n][:, t, i * P:(i + 1) * P] for i in range(4)])

                for b in range(FIRST_BLOCKS):
                    for t in range(TILES):
                        project(b, t)
                pe.wait_ge(sem("params_loaded"), 16 * N_PARAMS * (l + 1))
                transposes(("wsT", l), [ws_raw[:, g, :] for g in range(BG)])

                for t in range(TILES):
                    pe.wait_ge(sem("qa_ready"), n_of(l, t) + 1)
                    transposes(("qTA", l, t), [aq[:, t, i * P:(i + 1) * P] for i in range(4)])
                pe.wait_ge(sem("ka_ready"), l + 1)
                for s in range(4):
                    transposes(("kTA", l, s), [k_dup[:, s, g, :] for g in range(AG)])
                for t in range(TILES):
                    wait_emptied(pe, "qTA", l, t)
                for s in range(4):
                    wait_emptied(pe, "kTA", l, s)
                n_a = len(A_UNITS)
                for i in range(n_a + LAG_V):
                    if i < n_a:
                        t, h = A_UNITS[i]
                        k0, nk = KEY_SLOTS[t][0] * P, len(KEY_SLOTS[t]) * P
                        half = slice(64 * (h % 2), 64 * (h % 2) + 64)
                        out = begin("sA", l, i)
                        done(pe.matmul(out[:, 0:nk], qTA[half, h // 2, t * P:(t + 1) * P],
                                       kTA[half, h // (AH // AG), k0:k0 + nk], start=True, stop=True), "sA", l, i)
                    if 0 <= i - LAG_T < n_a:
                        u = i - LAG_T
                        wait_emptied(pe, "sA", l, u)
                        transposes(("pTA", l, u), [pr[:, u % 6, j * P:(j + 1) * P]
                                                   for j in range(len(KEY_SLOTS[A_UNITS[u][0]]))])
                    if i >= LAG_V:
                        u = i - LAG_V
                        t, h = A_UNITS[u]
                        g = h // (AH // AG)
                        out = begin("oA", l, t) if h == 0 else bank[turn["oA", l, t][0]]
                        wait_emptied(pe, "pTA", l, u)
                        ks = KEY_SLOTS[t]
                        for j, s in enumerate(ks):
                            last = pe.matmul(out[:, h * AD:(h + 1) * AD], pt[:, u % 2, j * P:(j + 1) * P],
                                             akv[:, TILE_OF_KEY_SLOT[s], 128 + g * AD:128 + (g + 1) * AD],
                                             start=j == 0, stop=j == len(ks) - 1)
                        last.then_inc(sem("a_values_done"), 1)
                    if i in A_FILL:
                        project(*A_FILL[i])

                for t in range(TILES):
                    pe.wait_ge(sem("qd_ready"), n_of(l, t) + 1)
                    transposes(("qTD", l, t), [dq[:, t, i * P:(i + 1) * P] for i in range(4)])
                for s in range(4):
                    transposes(("kTD", l, s), [dk[:, TILE_OF_KEY_SLOT[s], i * P:(i + 1) * P] for i in range(4)])
                for t in range(TILES):
                    wait_emptied(pe, "qTD", l, t)
                for s in range(4):
                    wait_emptied(pe, "kTD", l, s)
                n_d = len(D_UNITS)
                for i in range(n_d + LAG_V):
                    if i < n_d:
                        t, h = D_UNITS[i]
                        k0, nk = KEY_SLOTS[t][0] * P, len(KEY_SLOTS[t]) * P
                        for j in range(2):
                            half = slice(64 * j, 64 * j + 64)
                            out = begin("sD", l, i, j)
                            done(pe.matmul(out[:, 0:nk], qTD[half, h, t * P:(t + 1) * P],
                                           kTD[half, h, k0:k0 + nk], start=True, stop=True), "sD", l, i, j)
                    if 0 <= i - LAG_T < n_d:
                        u = i - LAG_T
                        pe.wait_ge(sem("d_combined"), l * n_d + u + 1)
                        transposes(("pTD", l, u), [pr[:, (2 * u) % 6, j * P:(j + 1) * P]
                                                   for j in range(len(KEY_SLOTS[D_UNITS[u][0]]))])
                    if i >= LAG_V:
                        u = i - LAG_V
                        t, h = D_UNITS[u]
                        out = begin("oD", l, t) if h == 0 else bank[turn["oD", l, t][0]]
                        wait_emptied(pe, "pTD", l, u)
                        ks = KEY_SLOTS[t]
                        for j, s in enumerate(ks):
                            last = pe.matmul(out[:, h * DV:(h + 1) * DV], pt[:, u % 2, j * P:(j + 1) * P],
                                             dv[:, TILE_OF_KEY_SLOT[s], h * DV:(h + 1) * DV],
                                             start=j == 0, stop=j == len(ks) - 1)
                        last.then_inc(sem("d_values_done"), 1)
                    if i in D_FILL:
                        project(*D_FILL[i])

                wait_emptied(pe, "wsT", l)
                for t in range(TILES):
                    pe.wait_ge(sem("vn_ready"), n_of(l, t) + 1)
                    out = begin("bmm", l, t)
                    for g in range(BG):
                        last = pe.matmul(out[:, g * P:(g + 1) * P], wsT[:, g, :], bv[:, t, g * P:(g + 1) * P],
                                         start=True, stop=True)
                    done(last, "bmm", l, t)

                for t in range(TILES):
                    wait_emptied(pe, "proj", l, BLK["cq"], t)
                    wait_emptied(pe, "proj", l, BLK["ck"], t)
                for t in range(TILES):
                    transposes(("qTC", l, t), [cq[:, t, i * P:(i + 1) * P] for i in range(4)])
                for t in range(TILES):
                    transposes(("kTC", l, t), [ck[:, t, i * P:(i + 1) * P] for i in range(4)])
                for t in range(TILES):
                    wait_emptied(pe, "qTC", l, t)
                    wait_emptied(pe, "kTC", l, t)
                    out = begin("sC", l, t)
                    for h in range(CH):
                        last = pe.matmul(out[:, h * P:(h + 1) * P], qTC[:, h, t * P:(t + 1) * P],
                                         kTC[:, h, t * P:(t + 1) * P], start=True, stop=True)
                    done(last, "sC", l, t)
                for n, kind in ((0, "oA"), (1, "bmm")):
                    for t in range(TILES):
                        wait_emptied(pe, kind, l, t)
                    y_transposed(n)
                for b, t in LAST_FILL:
                    project(b, t)
                pe.wait_ge(sem("lf_ready"), l + 1)
                out = begin("cum", l)
                for a in range(2):
                    pe.matmul(out[:, 12 * a:12 * a + 12], tri[:, a, :], lf[:, a].rearrange("p t h -> p (t h)"),
                              start=True, stop=True)
                done(pe.matmul(out[:, 24:48], ones, lf.rearrange("p a t h -> p (a t h)"), start=True, stop=True),
                     "cum", l)
                pe.wait_ge(sem("yd_ready"), l + 1)
                y_transposed(3)
                for u, (t, a) in enumerate(C_UNITS):
                    nu = l * len(C_UNITS) + u
                    pe.wait_ge(sem("diag_ready"), nu + 1)
                    out = begin("rb", l, u)
                    done(pe.matmul(out, ones, diag.rearrange("p h s -> p (h s)"), start=True, stop=True), "rb", l, u)
                    for n, j in C_FILL[2 * u]:
                        merge(n, j)
                    pe.wait_ge(sem("w_ready"), nu + 1)
                    transposes(("wT", l, u), [Wc[:, h, :] for h in range(CH)])
                    if u in C_UPDATES:
                        pe.wait_ge(sem("kws_ready"), l * len(C_UPDATES) + u + 1)
                        for p2 in range(2):
                            out = begin("kv", l, u, p2)
                            for h in (2 * p2, 2 * p2 + 1):
                                o = 256 * (h % 2)
                                last = pe.matmul(out[:, o:o + CD + 1], kws[:, h, :], cv[:, t, h, :],
                                                 start=True, stop=True)
                            done(last, "kv", l, u, p2)
                    wait_emptied(pe, "wT", l, u)
                    for p2 in range(2):
                        out = begin("num", l, u, p2)
                        for h in (2 * p2, 2 * p2 + 1):
                            o = 256 * (h % 2)
                            last = pe.matmul(out[:, o:o + CD + 1], WT[:, h, :], cv[:, t, h, :], start=True, stop=True)
                        done(last, "num", l, u, p2)
                    if t:
                        if u >= 4:
                            pe.wait_ge(sem("state_ready"), 2 * l + u - 3)
                        for p2 in range(2):
                            out = begin("qC", l, u, p2)
                            for h in (2 * p2, 2 * p2 + 1):
                                o = 256 * (h % 2)
                                last = pe.matmul(out[:, o:o + CD + 1], qTC[:, h, t * P:(t + 1) * P],
                                                 c_state[:, a, h, :], start=True, stop=True)
                            done(last, "qC", l, u, p2)

                    for n, j in C_FILL[2 * u + 1]:
                        merge(n, j)
                for n, j in NORM_MERGES:
                    merge(n, j)
                pe.wait_ge(sem("yc_ready"), l + 1)
                y_transposed(2)
                keys = slot(pe, "keys", l)[:, 0:16 * PQ].rearrange("p (b d) -> p b d", b=16)
                for i in range(4):
                    transposes(("kT", l, i), [keys[:, 4 * i + k, :] for k in range(4)])
                for n, j in LAST_MERGES:
                    merge(n, j)
                pe.wait_ge(sem("merged_ready"), l + 1)

                def output(t):
                    for hf in range(2):
                        wo = slot(pe, "out", l, hf).rearrange("p (c n) -> p c n", c=KC)
                        out = begin("out", l, hf, t)
                        for k in range(KC):
                            last = pe.matmul(out, merged[:, k, t * P:(t + 1) * P], wo[:, k, :],
                                             start=k == 0, stop=k == KC - 1)
                        done(last, "out", l, hf, t)

                def x_transposed(t):
                    pe.wait_ge(sem("x_mid"), n_of(l, t) + 1)
                    for hf in range(2):
                        transposes(("x2T", l, t, hf), [x[:, t, (4 * hf + i) * P:(4 * hf + i + 1) * P] for i in range(4)])

                def h_rows(t):
                    for hf in range(2):
                        wait_emptied(pe, "x2T", l, t, hf)
                        transposes(("h2", l, t, hf), [hT[:, 4 * hf + i, t * P:(t + 1) * P] for i in range(4)])

                def query_weights(k):
                    i = Q_ORDER.index(k)
                    if i in (0, 3):
                        return slot(pe, "q", l, k).rearrange("p (c n) -> p c n", c=KC)
                    pe.wait_ge(sem(f"q_extra{i - 1}_loaded"), 16 * (l + 1))
                    return q_extra[:, i - 1, :].rearrange("p (c n) -> p c n", c=KC)

                def first_queries(c4):
                    wq = query_weights(c4)
                    out = begin("q0", l, c4)
                    for i in range(4):
                        for k in range(KC):
                            last = pe.matmul(out[:, i * P:(i + 1) * P], wq[:, k, i * P:(i + 1) * P], hT[:, k, 0:P],
                                             start=k == 0, stop=k == KC - 1)
                    done(last, "q0", l, c4)

                def scores(t, groups=range(4)):
                    for i in groups:
                        for k in range(4):
                            if t == 0:
                                wait_emptied(pe, "q0", l, i)
                            else:
                                wait_emptied(pe, "q", l, 4 * i + k)
                        out = begin("sc", l, t, i)
                        for k in range(4):
                            last = pe.matmul(out[:, k * P:(k + 1) * P], qTp[:, 4 * i + k, t * P:(t + 1) * P],
                                             keysT[:, 4 * i + k, :], start=True, stop=True)
                        done(last, "sc", l, t, i)

                output(0)
                output(1)
                x_transposed(0)
                h_rows(0)
                output(2)
                x_transposed(1)
                for k in Q_ORDER[:2]:
                    first_queries(k)
                x_transposed(2)
                for i in range(4):
                    wait_emptied(pe, "kT", l, i)
                scores(0, Q_ORDER[:2])
                for i in (2, 3):
                    first_queries(Q_ORDER[i])
                    h_rows(i - 1)
                    scores(0, Q_ORDER[i:i + 1])
                for j in Q_HEADS:
                    wq = query_weights(j // 4)
                    out = begin("q", l, j)
                    for k in range(KC):
                        last = pe.matmul(out[:, 0:2 * P], wq[:, k, (j % 4) * P:(j % 4 + 1) * P], hT[:, k, P:T],
                                         start=k == 0, stop=k == KC - 1)
                    done(last, "q", l, j)
                scores(1)
                if l + 1 < DEPTH:
                    modulation(l + 1)
                scores(2)
                for t in range(TILES - 1):
                    n = n_of(l, t)
                    out = [begin("vsum", l, t, hf) for hf in range(2)]
                    pe.wait_ge(sem("weights_spread"), l * (TILES - 1) + t + 1)
                    for c8 in range(PE_ROUNDS):
                        for j in range(SLOTS):
                            i = c8 * SLOTS + j
                            pe.wait_ge(sem(f"row{j}_loaded"), (2 * n * ROUNDS + ROUNDS + c8 + 1) * 16)
                            for hf in range(2):
                                last = pe.matmul(out[hf], spread_w[:, i, :], rows[:, j, hf * 512:(hf + 1) * 512],
                                                 start=i == 0, stop=i == PE_PICKS - 1)
                            last.then_inc(sem("rows_free"), 1)
                    pe.wait_ge(sem("rows_free"), (2 * n + 1) * PICKS + SLOTS + PE_PICKS)
                    pe.sem_inc(sem("v_summed"), 1)
            assert at[0] == len(jobs)

        @block.scalar
        def _(act):
            steps = [0]

            def step(ins):
                ins.then_inc(sem("act_steps"), 1)
                steps[0] += 1
                act.wait_ge(sem("act_steps"), steps[0])

            def copy_out(job, dst, width=512, scale=None):
                src = wait_filled(act, *job)[:, 0:width]
                if len(dst.shape) == 3:
                    src = src.rearrange("p (a b) -> p a b", a=dst.shape[1])
                if scale is None:
                    empties(act, act.copy(dst, src), *job)
                else:
                    empties(act, act.mul(dst, src, scale), *job)

            def modulation(l):
                if l:
                    act.wait_ge(sem("x_mixed"), 2 * TILES * l)
                for j in range(MODS):
                    src = wait_filled(act, "mod", l, j)
                    if j >= 2 or l:
                        act.wait_ge(sem(f"mod_stored{j % 2}"), 16 * (MODS // 2 * l + j // 2))
                        jj, ll = (j - 2, l) if j >= 2 else (MODS - 2 + j, l - 1)
                        if jj // 2 in (0, 1, 3, 4):
                            wait_filled(act, "mcol", ll, jj)
                    empties(act, act.copy(m_stage[:, j % 2, :], src[0:2, :]), "mod", l, j)
                    act.dma_start(mod_dram[l, :, j * 512:(j + 1) * 512], m_stage[:, j % 2, :])\
                       .then_inc(sem(f"mod_stored{j % 2}"), 16)
                    if j // 2 in (0, 1, 3, 4):
                        src = wait_filled(act, "mcol", l, j)
                        a = {0: 0, 1: 1, 3: 2, 4: 3}[j // 2]
                        dst = modcol[:, l, a, 4 * (j % 2):4 * (j % 2) + 4, :].rearrange("p c n -> p (c n)")
                        if a % 2:
                            last = act.activation(dst, src[:, 0:8], ACT.Identity, bias=1.0)
                        else:
                            last = act.copy(dst, src[:, 0:8])
                        empties(act, last, "mcol", l, j)

            act.wait_ge(sem("cond_loaded"), 32)
            act.activation(silu_c, cond_raw, ACT.Sigmoid).then_inc(sem("cond_sigmoid"), 1)
            modulation(0)
            for l in range(DEPTH):
                def project(b, t):
                    name, _, w = BLOCKS[b]
                    job = ("proj", l, b, t)
                    if name == "cg":
                        copy_out(job, cg[:, t, :], 16)
                    elif name == "ck":
                        copy_out(job, ck[:, t, :], 512, CD ** -0.5)
                    elif name == "cv":
                        copy_out(job, cv[:, t, :, 0:CD])
                    elif name == "co":
                        src = wait_filled(act, *job)
                        empties(act, act.activation(co[:, t, :], src, ACT.Sigmoid), *job)
                    else:
                        copy_out(job, {"aq": aq, "akv": akv, "dq": dq, "dk": dk, "dv": dv, "bu": bu,
                                       "bv": bv, "cq": cq}[name][:, t, :], w)

                def merge(n, j):
                    at = MERGES.index((n, j))
                    src = wait_filled(act, "gate", l, n, j)
                    if at >= 2:
                        act.wait_ge(sem("sg_used"), l * len(MERGES) + at - 1)
                    empties(act, act.activation(sg[:, j % 2, :], src[:, 0:T], ACT.Sigmoid), "gate", l, n, j)

                for b in range(FIRST_BLOCKS):
                    for t in range(TILES):
                        project(b, t)
                copy_out(("wsT", l), wsT)
                for t in range(TILES):
                    copy_out(("qTA", l, t), qTA[:, :, t * P:(t + 1) * P])
                for s in range(4):
                    copy_out(("kTA", l, s), kTA[:, :, s * P:(s + 1) * P], 256)
                for i in range(2):
                    act.wait_ge(sem(f"mod_stored{i}"), 16 * MODS // 2 * (l + 1))
                n_a = len(A_UNITS)
                for i in range(n_a):
                    t, h = A_UNITS[i]
                    nk = len(KEY_SLOTS[t]) * P
                    if i >= 6:
                        wait_filled(act, "pTA", l, i - 6)
                    act.wait_ge(sem("a_negmax"), l * n_a + i + 1)
                    src = wait_filled(act, "sA", l, i)
                    step(act.activation(pr[:, i % 6, 0:nk], src[:, 0:nk], ACT.Exp, bias=negm[:, i:i + 1],
                                        scale=AD ** -0.5, accum_out=sums[:, i:i + 1]))
                    act.sem_inc(emptied[turn["sA", l, i][0]], 1)
                    if i in A_FILL:
                        project(*A_FILL[i])
                for i in range(n_a, n_a + LAG_V):
                    if i in A_FILL:
                        project(*A_FILL[i])
                for t in range(TILES):
                    copy_out(("qTD", l, t), qTD[:, :, t * P:(t + 1) * P])
                for s in range(4):
                    copy_out(("kTD", l, s), kTD[:, :, s * P:(s + 1) * P])
                act.wait_ge(sem("lam_sums"), l + 1)
                step(act.activation(lam_e, lam_e, ACT.Exp))
                act.sem_inc(sem("lam_exps"), 1)
                n_d = len(D_UNITS)
                for i in range(n_d + LAG_T):
                    if i < n_d:
                        t, h = D_UNITS[i]
                        nk = len(KEY_SLOTS[t]) * P
                        if i >= 3:
                            wait_filled(act, "pTD", l, i - 3)
                        else:
                            wait_filled(act, "pTA", l, n_a - 1)
                        for j in range(2):
                            act.wait_ge(sem("d_negmax"), 2 * (l * n_d + i) + j + 1)
                            src = wait_filled(act, "sD", l, i, j)
                            step(act.activation(pr[:, (2 * i + j) % 6, 0:nk], src[:, 0:nk], ACT.Exp,
                                                bias=negm[:, 2 * i + j:2 * i + j + 1], scale=DD ** -0.5,
                                                accum_out=sums[:, 2 * i + j:2 * i + j + 1]))
                            act.sem_inc(emptied[turn["sD", l, i, j][0]], 1)
                    if i >= LAG_T:
                        u = i - LAG_T
                        nk = len(KEY_SLOTS[D_UNITS[u][0]]) * P
                        if u >= 2:
                            act.wait_ge(sem("d_values_done"), l * n_d + u - 1)
                        else:
                            act.wait_ge(sem("a_values_done"), (l + 1) * n_a)
                        copy_out(("pTD", l, u), pt[:, u % 2, 0:nk], nk)
                    if i in D_FILL:
                        project(*D_FILL[i])
                for t in range(TILES):
                    copy_out(("qTC", l, t), qTC[:, :, t * P:(t + 1) * P])
                for t in range(TILES):
                    copy_out(("kTC", l, t), kTC[:, :, t * P:(t + 1) * P])
                for t in range(TILES):
                    copy_out(("sC", l, t), sC[:, t, :])
                for n in (0, 1):
                    for t in range(TILES):
                        copy_out(("yT", l, n, t), yT[n][:, :, t * P:(t + 1) * P])
                act.wait_ge(sem("lf_abs"), l + 1)
                step(act.activation(lt, lt, ACT.Exp, scale=-1.0))
                step(act.activation(lt, lt, ACT.Ln, bias=1.0))
                act.sem_inc(sem("lf_log"), 1)
                for b, t in LAST_FILL:
                    project(b, t)
                for t in range(TILES):
                    copy_out(("yT", l, 3, t), yT[3][:, :, t * P:(t + 1) * P])
                for u, (t, a) in enumerate(C_UNITS):
                    nu = l * len(C_UNITS) + u
                    act.wait_ge(sem("exp_args"), nu + 1)
                    act.activation(se, se, ACT.Exp)
                    step(act.activation(Mx, Mx, ACT.Exp))
                    act.sem_inc(sem("exps_ready"), 1)
                    for n, j in C_FILL[2 * u]:
                        merge(n, j)
                    copy_out(("wT", l, u), WT)
                    if u < 2:
                        for p2 in range(2):
                            src = wait_filled(act, "kv", l, u, p2).rearrange("p (h e) -> p h e", h=2)[:, :, 0:CD + 1]
                            empties(act, act.copy(c_new[:, a, 2 * p2:2 * p2 + 2, :], src), "kv", l, u, p2)
                        act.sem_inc(sem("c_new_ready"), 1)
                    if u:
                        act.wait_ge(sem("nd_used"), nu)
                    for p2 in range(2):
                        src = wait_filled(act, "num", l, u, p2).rearrange("p (h e) -> p h e", h=2)[:, :, 0:CD + 1]
                        empties(act, act.copy(ND[:, 2 * p2:2 * p2 + 2, :], src), "num", l, u, p2)
                    for n, j in C_FILL[2 * u + 1]:
                        merge(n, j)
                for n, j in NORM_MERGES:
                    merge(n, j)
                for t in range(TILES):
                    copy_out(("yT", l, 2, t), yT[2][:, :, t * P:(t + 1) * P])
                for i in range(4):
                    copy_out(("kT", l, i), keysT[:, 4 * i:4 * i + 4, :])
                for n, j in LAST_MERGES:
                    merge(n, j)

                def h_rows(t):
                    for hf in range(2):
                        copy_out(("h2", l, t, hf), h2[:, t, hf * 512:(hf + 1) * 512])

                def scores(t, groups=range(4)):
                    for i in groups:
                        copy_out(("sc", l, t, i), S[:, 4 * i:4 * i + 4, :])

                def gate_exps(t):
                    act.wait_ge(sem("gate_args"), n_of(l, t) + 1)
                    step(act.activation(best, best, ACT.Exp))
                    act.sem_inc(sem("gate_exps"), 1)

                act.wait_ge(sem("kv_stored"), 64 * (l + 1))
                h_rows(0)
                for i, k in enumerate(Q_ORDER):
                    copy_out(("q0", l, k), qTp[:, 4 * k:4 * k + 4, 0:P])
                    if i == 1:
                        scores(0, Q_ORDER[:2])
                    elif i >= 2:
                        h_rows(i - 1)
                        scores(0, Q_ORDER[i:i + 1])
                for i, j in enumerate(Q_HEADS):
                    if i == GATE_AT:
                        gate_exps(0)
                    copy_out(("q", l, j), qTp[:, j, P:T], 2 * P)
                for t in range(TILES):
                    if t + 1 < TILES:
                        act.wait_ge(sem("scores_used"), n_of(l, t) + 1)
                        scores(t + 1)
                    if t:
                        gate_exps(t)
                    elif l + 1 < DEPTH:
                        modulation(l + 1)
                    act.wait_ge(sem("dots_ready"), n_of(l, t) + 1)
                    step(act.activation(act_a, act_a, ACT.Gelu))
                    act.sem_inc(sem("gelu_ready"), 1)

        @block.vector
        def _(v):
            steps = [0]

            def step(ins):
                ins.then_inc(sem("vec_steps"), 1)
                steps[0] += 1
                v.wait_ge(sem("vec_steps"), steps[0])

            roots = [0]

            def inv_sqrt(n):
                v.sem_inc(sem("squares_ready"), 1)
                roots[0] += 1
                v.wait_ge(sem("roots_ready"), roots[0])

            def bc(ap, shape, axis):
                return ap.unsqueeze(axis).to_broadcast(shape)

            def rope(src, n, t):
                s5 = src.rearrange("p (n a b c) -> p n a b c", n=n, a=2, b=2)
                t5 = tmp[:, 0:n * 64].rearrange("p (n a b c) -> p n a b c", n=n, a=2, b=2)
                sn = rope_cs[:, 1, t, :].rearrange("p (a b c) -> p a b c", a=2, b=2)
                for b in range(2):
                    last = v.tensor_tensor(t5[:, :, :, b, :], s5[:, :, :, 1 - b, :],
                                           bc(sn[:, :, b, :], [P, n, 2, 16], 1), ALU.mult)
                step(last)
                s3 = src.rearrange("p (n d) -> p n d", n=n)
                step(v.tensor_tensor(s3, s3, bc(rope_cs[:, 0, t, :], [P, n, 64], 1), ALU.mult))
                step(v.tensor_tensor(src, src, tmp[:, 0:n * 64], ALU.add))

            def rms_heads(src, n, d):
                s3 = src.rearrange("p (n d) -> p n d", n=n)
                step(v.tensor_tensor(tmp[:, 0:n * d], src, src, ALU.mult))
                step(v.tensor_reduce(ms[:, 0:n], tmp[:, 0:n * d].rearrange("p (n d) -> p n d", n=n), X, ALU.add))
                step(v.tensor_scalar(ms[:, 0:n], ms[:, 0:n], 1.0 / d, EPS, ALU.mult, ALU.add))
                inv_sqrt(n)
                step(v.tensor_tensor(s3, s3, bc(rs[:, 0:n], [P, n, d], 2), ALU.mult))

            def modulate(job, l, t, hf, which):
                src = wait_filled(v, *job)
                cond = 0 if t == 0 else 1
                for i in range(4):
                    k = 4 * hf + i
                    last = v.tensor_scalar(hT[:, k, t * P:(t + 1) * P], src[:, i * P:(i + 1) * P],
                                           modcol[:, l, which + 1, k, cond:cond + 1],
                                           modcol[:, l, which, k, cond:cond + 1], ALU.mult, ALU.add)
                empties(v, last, *job)

            def layer_norm(xt, lg, lb):
                for i in range(2):
                    last = v.bn_stats(stats[:, i, :], xt[:, i * 512:(i + 1) * 512])
                step(last)
                step(v.bn_aggr(aggr[:, 0, :], stats[:, 0:2, :].rearrange("p a s -> p (a s)")))
                step(v.tensor_scalar(ms[:, 0:1], aggr[:, 0, 1:2], EPS, None, ALU.add))
                inv_sqrt(1)
                step(v.tensor_scalar(xt, xt, aggr[:, 0, 0:1], rs[:, 0:1], ALU.subtract, ALU.mult))
                step(v.tensor_tensor(xt, xt, lg, ALU.mult))
                step(v.tensor_tensor(xt, xt, lb, ALU.add))

            v.memset(small[:, 468:472], 0.0)
            v.wait_ge(sem("cond_sigmoid"), 1)
            v.tensor_tensor(silu_c, silu_c, cond_raw, ALU.mult).then_inc(sem("silu_ready"), 1)
            v.wait_ge(sem("consts_loaded"), 16)
            v.wait_ge(sem("ms_set"), 1)
            for l in range(DEPTH):
                lam_init = 0.8 - 0.6 * math.exp(-0.3 * l)
                for t in range(TILES):
                    for hf in range(2):
                        modulate(("xT", l, t, hf), l, t, hf, 0)
                step(v.memset(cv[:, :, :, CD], 1.0))
                v.wait_ge(sem("params_loaded"), 16 * N_PARAMS * (l + 1))
                step(v.tensor_tensor(tmp[:, 0:128].rearrange("p (a d) -> p a d", a=2), lam_v[:, :, 0, :],
                                     lam_v[:, :, 1, :], ALU.mult))
                step(v.tensor_reduce(lam_e, tmp[:, 0:128].rearrange("p (a d) -> p a d", a=2), X, ALU.add))
                v.sem_inc(sem("lam_sums"), 1)

                for t in range(TILES):
                    wait_emptied(v, "proj", l, BLK["aq"], t)
                    rms_heads(aq[:, t, :], AH, AD)
                    q3 = aq[:, t, :].rearrange("p (n d) -> p n d", n=AH)
                    step(v.tensor_tensor(q3, q3, bc(gains[:, 0, :], [P, AH, AD], 1), ALU.mult))
                    if t:
                        rope(aq[:, t, :], AH, t - 1)
                    v.sem_inc(sem("qa_ready"), 1)
                for t in range(TILES):
                    wait_emptied(v, "proj", l, BLK["akv"], t)
                    ak = akv[:, t, 0:128]
                    rms_heads(ak, AG, AD)
                    k3 = ak.rearrange("p (n d) -> p n d", n=AG)
                    step(v.tensor_tensor(k3, k3, bc(gains[:, 1, :], [P, AG, AD], 1), ALU.mult))
                    if t:
                        rope(ak, AG, t - 1)
                    else:
                        v.sem_inc(sem("ak_ready"), 1)
                for s in range(4):
                    k3 = akv[:, TILE_OF_KEY_SLOT[s], 0:128].rearrange("p (g d) -> p g d", g=AG)
                    for r in range(2):
                        last = v.tensor_copy(k_dup[:, s, :, r * 64:(r + 1) * 64], k3)
                step(last)
                v.sem_inc(sem("ka_ready"), 1)
                for t in range(TILES):
                    wait_emptied(v, "proj", l, BLK["dq"], t)
                    wait_emptied(v, "proj", l, BLK["dk"], t)
                    if t:
                        rope(dq[:, t, :], 8, t - 1)
                        rope(dk[:, t, :], 8, t - 1)
                    v.sem_inc(sem("qd_ready"), 1)
                n_a = len(A_UNITS)
                for i in range(n_a + LAG_V):
                    if i < n_a:
                        nk = len(KEY_SLOTS[A_UNITS[i][0]]) * P
                        src = wait_filled(v, "sA", l, i)
                        step(v.reduce_max(negm[:, i:i + 1], src[:, 0:nk], X))
                        v.tensor_scalar(negm[:, i:i + 1], negm[:, i:i + 1], -(AD ** -0.5), None, ALU.mult)\
                         .then_inc(sem("a_negmax"), 1)
                    if 0 <= i - LAG_T < n_a:
                        u = i - LAG_T
                        nk = len(KEY_SLOTS[A_UNITS[u][0]]) * P
                        src = wait_filled(v, "pTA", l, u)
                        if u >= 2:
                            v.wait_ge(sem("a_values_done"), l * n_a + u - 1)
                        empties(v, v.tensor_copy(pt[:, u % 2, 0:nk], src[:, 0:nk]), "pTA", l, u)
                    if i >= LAG_V and A_UNITS[i - LAG_V][1] == AH - 1:
                        t = A_UNITS[i - LAG_V][0]
                        v.wait_ge(sem("a_values_done"), l * n_a + (t + 1) * AH)
                        src = bank[turn["oA", l, t][0]]
                        step(v.reciprocal(rsum[:, 0:AH], sums[:, t * AH:(t + 1) * AH]))
                        empties(v, v.tensor_tensor(yA[:, t, :].rearrange("p (h d) -> p h d", h=AH),
                                                   src.rearrange("p (h d) -> p h d", h=AH),
                                                   bc(rsum[:, 0:AH], [P, AH, AD], 2), ALU.mult), "oA", l, t)

                v.wait_ge(sem("lam_exps"), l + 1)
                step(v.tensor_tensor(neg_lam, lam_e[:, 1:2], lam_e[:, 0:1], ALU.subtract))
                step(v.tensor_scalar(neg_lam, neg_lam, -lam_init, None, ALU.add))
                n_d = len(D_UNITS)
                for i in range(n_d + LAG_V):
                    if i < n_d:
                        nk = len(KEY_SLOTS[D_UNITS[i][0]]) * P
                        for j in range(2):
                            src = wait_filled(v, "sD", l, i, j)
                            m = negm[:, 2 * i + j:2 * i + j + 1]
                            step(v.reduce_max(m, src[:, 0:nk], X))
                            v.tensor_scalar(m, m, -(DD ** -0.5), None, ALU.mult).then_inc(sem("d_negmax"), 1)
                    if 0 <= i - 1 < n_d:
                        u = i - 1
                        nk = len(KEY_SLOTS[D_UNITS[u][0]]) * P
                        wait_emptied(v, "sD", l, u, 0)
                        wait_emptied(v, "sD", l, u, 1)
                        r = rsum[:, 0:2]
                        step(v.reciprocal(r, sums[:, 2 * u:2 * u + 2]))
                        step(v.tensor_tensor(r[:, 1:2], r[:, 1:2], neg_lam, ALU.mult))
                        p0, p1 = pr[:, (2 * u) % 6, 0:nk], pr[:, (2 * u + 1) % 6, 0:nk]
                        step(v.tensor_scalar(p0, p0, r[:, 0:1], None, ALU.mult))
                        step(v.scalar_tensor_tensor(out=p0, in0=p1, scalar=r[:, 1:2], in1=p0, op0=ALU.mult,
                                                    op1=ALU.add))
                        v.sem_inc(sem("d_combined"), 1)
                    if i >= LAG_V and D_UNITS[i - LAG_V][1] == DH - 1:
                        t = D_UNITS[i - LAG_V][0]
                        v.wait_ge(sem("d_values_done"), l * n_d + (t + 1) * DH)
                        if t == 0:
                            v.wait_ge(sem("kv_stored"), 64 * (l + 1))
                            for s in range(4):
                                wait_filled(v, "kTD", l, s)
                        empties(v, v.tensor_copy(yD[:, t, :], bank[turn["oD", l, t][0]]), "oD", l, t)
                for t in range(TILES):
                    wait_emptied(v, "proj", l, BLK["bv"], t)
                    step(v.bn_stats(stats[:, 0, :], bv[:, t, :]))
                    step(v.bn_aggr(aggr[:, 0, :], stats[:, 0, :]))
                    step(v.tensor_scalar(ms[:, 0:1], aggr[:, 0, 1:2], EPS, None, ALU.add))
                    inv_sqrt(1)
                    step(v.tensor_scalar(bv[:, t, :], bv[:, t, :], aggr[:, 0, 0:1], rs[:, 0:1],
                                         ALU.subtract, ALU.mult))
                    v.sem_inc(sem("vn_ready"), 1)
                for t in range(TILES):
                    src = wait_filled(v, "bmm", l, t)
                    wait_emptied(v, "proj", l, BLK["bu"], t)
                    for g in range(BG):
                        cols = slice(g * P, (g + 1) * P)
                        last = v.scalar_tensor_tensor(out=yB[:, t, cols], in0=src[:, cols], scalar=b_bias[:, g:g + 1],
                                                      in1=bu[:, t, cols], op0=ALU.add, op1=ALU.mult)
                    empties(v, last, "bmm", l, t)

                for t in range(TILES):
                    rms_heads(yD[:, t, :], DH, DV)
                    step(v.scalar_tensor_tensor(out=yD[:, t, :], in0=yD[:, t, :], scalar=1.0 - lam_init, in1=dgn,
                                                op0=ALU.mult, op1=ALU.mult))

                v.sem_inc(sem("yd_ready"), 1)
                for t in range(TILES):
                    wait_emptied(v, "proj", l, BLK["cg"], t)
                step(v.tensor_tensor(cg, cg, bc(cg_bias, [P, TILES, 16], 1), ALU.add))
                g5 = cg.rearrange("p t (a k h) -> p a k t h", a=2, k=2)
                for a in range(2):
                    last = v.tensor_scalar(lf[:, a], g5[:, a, 1], -1.0, None, ALU.mult)
                step(last)
                for a in range(2):
                    last = v.tensor_tensor(lt[:, a], lf[:, a], g5[:, a, 1], ALU.max)
                step(last)
                v.sem_inc(sem("lf_abs"), 1)
                v.wait_ge(sem("lf_log"), l + 1)
                for a in range(2):
                    last = v.scalar_tensor_tensor(out=lf[:, a], in0=g5[:, a, 1], scalar=0.0, in1=lt[:, a],
                                                  op0=ALU.min, op1=ALU.subtract)
                step(last)
                v.sem_inc(sem("lf_ready"), 1)
                src = wait_filled(v, "cum", l)
                empties(v, v.tensor_copy(csum.rearrange("p k a t h -> p (k a t h)"), src[:, 0:48]), "cum", l)
                for a in range(2):
                    last = v.tensor_tensor(rr[:, a], g5[:, a, 0], csum[:, 0, a], ALU.subtract)
                step(last)
                for t in range(TILES):
                    wait_emptied(v, "sC", l, t)
                    wait_filled(v, "pTD", l, n_d - 1)
                def merge(n, j):
                    wait_emptied(v, "gate", l, n, j)
                    src = wait_filled(v, "br", l, n, j)[:, 0:T]
                    dst = merged[:, j, :] if n == MERGE_ORDER[0] else prod
                    empties(v, v.tensor_tensor(dst, src, sg[:, j % 2, :], ALU.mult), "br", l, n, j)
                    v.sem_inc(sem("sg_used"), 1)
                    if n != MERGE_ORDER[0]:
                        step(v.tensor_tensor(merged[:, j, :], merged[:, j, :], prod, ALU.add))

                def spread(u):
                    t, a = C_UNITS[u]
                    step(v.tensor_tensor(diag, bc(ident, [P, CH, P], 1), bc(rr[:, a, t, :], [P, CH, P], 2),
                                         ALU.mult))
                    v.sem_inc(sem("diag_ready"), 1)

                spread(0)
                for u, (t, a) in enumerate(C_UNITS):
                    nu = l * len(C_UNITS) + u
                    r = rr[:, a, t, :]
                    m = m_lat[:, a, :] if t else zero4
                    src = wait_filled(v, "rb", l, u).rearrange("p (h s) -> p h s", h=CH)
                    step(v.tensor_tensor(Mx, src, bc(negmask[:, a, :], [P, CH, P], 1), ALU.add))
                    v.tensor_reduce(mxr, Mx, X, ALU.max)
                    empties(v, v.tensor_reduce(mra, src, X, ALU.max), "rb", l, u)
                    v.tensor_tensor(mxl, mra, m, ALU.max)
                    step(v.tensor_tensor(mxr, mxr, m, ALU.max))
                    v.tensor_tensor(Mx, Mx, bc(mxr, [P, CH, P], 2), ALU.subtract)
                    v.tensor_tensor(se[:, 0, :], m, mxr, ALU.subtract)
                    v.scalar_tensor_tensor(out=se[:, 1, :], in0=csum[:, 0, a, t, :], scalar=-1.0, in1=mxr,
                                           op0=ALU.mult, op1=ALU.subtract)
                    v.tensor_tensor(se[:, 2, :], m, mxl, ALU.subtract)
                    step(v.tensor_tensor(se[:, 3, :], r, mxl, ALU.subtract))
                    v.sem_inc(sem("exp_args"), 1)
                    if u in C_UPDATES:
                        dst = m_lat[:, a, :] if t else m_out[:, a, :]
                        step(v.tensor_tensor(dst, csum[:, 1, a, t, :], mxl, ALU.add))
                    v.wait_ge(sem("exps_ready"), nu + 1)
                    step(v.tensor_tensor(Wc, sC[:, t, :].rearrange("p (h s) -> p h s", h=CH), Mx, ALU.mult))
                    v.sem_inc(sem("w_ready"), 1)
                    if u in C_UPDATES:
                        step(v.tensor_tensor(kws, ck[:, t, :].rearrange("p (h d) -> p h d", h=CH),
                                             bc(se[:, 3, :], [P, CH, CD], 2), ALU.mult))
                        v.sem_inc(sem("kws_ready"), 1)
                    for n, j in C_FILL[2 * u]:
                        merge(n, j)
                    wait_emptied(v, "num", l, u, 0)
                    wait_emptied(v, "num", l, u, 1)
                    if t:
                        for p2 in range(2):
                            src = wait_filled(v, "qC", l, u, p2)
                            for h in (2 * p2, 2 * p2 + 1):
                                o = 256 * (h % 2)
                                last = v.scalar_tensor_tensor(out=ND[:, h, :], in0=src[:, o:o + CD + 1],
                                                              scalar=se[:, 0, h:h + 1], in1=ND[:, h, :],
                                                              op0=ALU.mult, op1=ALU.add)
                            empties(v, last, "qC", l, u, p2)
                    if u in (2, 3):
                        for p2 in range(2):
                            src = wait_filled(v, "kv", l, u, p2)
                            for h in (2 * p2, 2 * p2 + 1):
                                o = 256 * (h % 2)
                                last = v.scalar_tensor_tensor(out=c_state[:, a, h, :], in0=c_state[:, a, h, :],
                                                              scalar=se[:, 2, h:h + 1], in1=src[:, o:o + CD + 1],
                                                              op0=ALU.mult, op1=ALU.add)
                            empties(v, last, "kv", l, u, p2)
                        v.sem_inc(sem("state_ready"), 1)
                    step(v.tensor_scalar(dn[:, 0, :], ND[:, :, CD], -1.0, None, ALU.mult))
                    step(v.tensor_tensor(dn[:, 0, :], dn[:, 0, :], ND[:, :, CD], ALU.max))
                    step(v.tensor_tensor(dn[:, 0, :], dn[:, 0, :], se[:, 1, :], ALU.max))
                    step(v.reciprocal(dn[:, 1, :], dn[:, 0, :]))
                    y3 = yC[:, t, :].rearrange("p (h e) -> p h e", h=CH)
                    if C_FIRST[t] == u:
                        step(v.tensor_tensor(y3, ND[:, :, 0:CD], bc(dn[:, 1, :], [P, CH, CD], 2), ALU.mult))
                    else:
                        step(v.tensor_tensor(ND[:, :, 0:CD], ND[:, :, 0:CD], bc(dn[:, 1, :], [P, CH, CD], 2),
                                             ALU.mult))
                        step(v.tensor_tensor(y3, y3, ND[:, :, 0:CD], ALU.add))
                    v.sem_inc(sem("nd_used"), 1)
                    if u < 2:
                        wait_emptied(v, "kv", l, u, 0)
                        wait_emptied(v, "kv", l, u, 1)
                        if u == 1:
                            v.sem_inc(sem("m_out_ready"), 1)
                    if u + 1 < len(C_UNITS):
                        spread(u + 1)
                    for n, j in C_FILL[2 * u + 1]:
                        merge(n, j)
                for t in range(TILES):
                    y3 = yC[:, t, :].rearrange("p (h e) -> p h e", h=CH)
                    for h in range(CH):
                        last = v.bn_stats(stats[:, h, :], y3[:, h, :])
                    step(last)
                    for h in range(CH):
                        last = v.bn_aggr(aggr[:, h, :], stats[:, h, :])
                    step(last)
                    step(v.tensor_scalar(ms[:, 0:CH], aggr[:, :, 1], EPS, None, ALU.add))
                    inv_sqrt(CH)
                    for h in range(CH):
                        last = v.tensor_scalar(y3[:, h, :], y3[:, h, :], aggr[:, h, 0:1], rs[:, h:h + 1],
                                               ALU.subtract, ALU.mult)
                    step(last)
                    step(v.tensor_tensor(yC[:, t, :], yC[:, t, :], gn, ALU.mult))
                    wait_emptied(v, "proj", l, BLK["co"], t)
                    step(v.tensor_tensor(yC[:, t, :], yC[:, t, :], co[:, t, :], ALU.mult))
                    merge(*NORM_MERGES[t])
                v.sem_inc(sem("yc_ready"), 1)
                for n, j in LAST_MERGES:
                    merge(n, j)
                v.sem_inc(sem("merged_ready"), 1)
                v.wait_ge(sem("gl1_loaded"), 64 * (l + 1))

                def mix(t):
                    for hf in range(2):
                        cols = slice(hf * 512, (hf + 1) * 512)
                        src = wait_filled(v, "out", l, hf, t)
                        empties(v, v.tensor_tensor(z, src, gates1[:, 0 if t == 0 else 1, cols], ALU.mult),
                                "out", l, hf, t)
                        step(v.scalar_tensor_tensor(out=x[:, t, cols], in0=x[:, t, cols], scalar=ALPHA, in1=z,
                                                    op0=ALU.mult, op1=ALU.add))
                        v.sem_inc(sem("x_mixed"), 1)

                def norm(t):
                    layer_norm(x[:, t, :], ln1[0], ln1[1])
                    v.sem_inc(sem("x_mid"), 1)

                def modulated(t):
                    for hf in range(2):
                        modulate(("x2T", l, t, hf), l, t, hf, 2)

                mix(0)
                norm(0)
                mix(1)
                modulated(0)
                norm(1)
                mix(2)
                norm(2)
                modulated(1)
                modulated(2)
                v.wait_ge(sem("state_stored"), 16 * 5 * (l + 1))

                def pick_experts(t):
                    n = n_of(l, t)
                    r3 = rep.rearrange("p (b k) -> p b k", b=16)
                    for i in Q_ORDER:
                        wait_emptied(v, "sc", l, t, i)
                        group = range(4 * i, 4 * i + 4)
                        for b in group:
                            last = v.max(tops[:, b, 0:8], S[:, b, :])
                        step(last)
                        for b in group:
                            v.max_index(ixs_u[:, b, 0:8], tops[:, b, 0:8], S[:, b, :])
                            last = v.match_replace(r3[:, b, :], tops[:, b, 0:8], S[:, b, :], -3.0e38)
                        step(last)
                        for b in group:
                            last = v.max(tops[:, b, 8:16], r3[:, b, :])
                        step(last)
                        for b in group:
                            last = v.max_index(ixs_u[:, b, 8:16], tops[:, b, 8:16], r3[:, b, :])
                        step(last)
                    v.sem_inc(sem("scores_used"), 1)
                    step(v.tensor_copy(ixs_f, ixs_u))
                    t4 = tops.rearrange("p (h a) k -> p h a k", a=2)
                    c4 = cand.rearrange("p (h a b) -> p h a b", h=PH, a=PTOP)
                    step(v.tensor_tensor(c4, bc(t4[:, :, 0, :], [P, PH, PTOP, PTOP], 3),
                                         bc(t4[:, :, 1, :], [P, PH, PTOP, PTOP], 2), ALU.add))
                    c3 = cand.rearrange("p (h k) -> p h k", h=PH)
                    q3 = rep.rearrange("p (h k) -> p h k", h=PH)
                    for h in range(PH):
                        last = v.max(best[:, h, 0:8], c3[:, h, :])
                    step(last)
                    for h in range(PH):
                        v.max_index(pos[:, h, 0:8], best[:, h, 0:8], c3[:, h, :])
                        last = v.match_replace(q3[:, h, :], best[:, h, 0:8], c3[:, h, :], -3.0e38)
                    step(last)
                    for h in range(PH):
                        last = v.max(best[:, h, 8:16], q3[:, h, :])
                    step(last)
                    for h in range(PH):
                        last = v.max_index(pos[:, h, 8:16], best[:, h, 8:16], q3[:, h, :])
                    step(last)
                    r4 = rep.rearrange("p (h a b) -> p h a b", h=PH, a=PTOP)
                    x4 = ixs_f.rearrange("p (h a) k -> p h a k", a=2)
                    for a, dst in ((0, e_a), (1, e_b)):
                        if a == 0:
                            step(v.tensor_scalar(pos_p, pos, 4, None, ALU.logical_shift_right))
                        else:
                            step(v.tensor_scalar(pos_p, pos, 15, None, ALU.bitwise_and))
                        step(v.tensor_copy(pos_f, pos_p))
                        step(v.tensor_tensor(r4, bc(pos_f, [P, PH, PTOP, PTOP], 3),
                                             iota16.unsqueeze(1).unsqueeze(1).to_broadcast([P, PH, PTOP, PTOP]),
                                             ALU.is_equal))
                        step(v.tensor_tensor(r4, r4, bc(x4[:, :, a, :], [P, PH, PTOP, PTOP], 2), ALU.mult))
                        step(v.tensor_reduce(dst, r4, X, ALU.add))
                    step(v.tensor_scalar(e_a, e_a, float(PKEYS), float(l * EXPERTS), ALU.mult, ALU.add))
                    step(v.tensor_tensor(idx[:, n % 2, :].rearrange("p (h k) -> p h k", h=PH), e_a, e_b, ALU.add))
                    v.sem_inc(sem("idx_ready"), 1)
                    step(v.tensor_copy(gmax, best[:, :, 0]))
                    step(v.tensor_tensor(best, best, bc(gmax, [P, PH, PTOP], 2), ALU.subtract))
                    v.sem_inc(sem("gate_args"), 1)
                    v.wait_ge(sem("gate_exps"), n + 1)
                    step(v.tensor_reduce(gmax, best, X, ALU.add))
                    step(v.reciprocal(gmax, gmax))
                    step(v.tensor_tensor(best, best, bc(gmax, [P, PH, PTOP], 2), ALU.mult))

                pick_experts(0)
                for t in range(TILES):
                    n = n_of(l, t)
                    used0 = 2 * PICKS * n
                    if n == 0:
                        v.sem_inc(sem("rows_free"), SLOTS)
                    with v.Fori(0, ROUNDS // 2) as k:
                        for half in range(2):
                            c8 = k * 2 + half
                            for j in range(SLOTS):
                                v.wait_ge(sem(f"row{j}_loaded"), (c8 + (2 * n * ROUNDS + 1)) * 16)
                                v.tensor_tensor_reduce(out=rows[:, j, :], in0=rows[:, j, :], in1=h2[:, t, :],
                                                       scale=1.0, scalar=0.0, op0=ALU.mult, op1=ALU.add,
                                                       accum_out=dots[:, half, j:j + 1])\
                                 .then_inc(sem("rows_free"), 1)
                            v.wait_ge(sem("rows_free"), c8 * SLOTS + (used0 + 2 * SLOTS))
                            v.tensor_copy(act_a[:, bass.ds(c8 * SLOTS, SLOTS)], dots[:, half, :])\
                             .then_inc(sem("dots_kept"), 1)
                            v.wait_ge(sem("dots_kept"), c8 + (n * ROUNDS + 1))
                    v.sem_inc(sem("dots_ready"), 1)
                    v.wait_ge(sem("gelu_ready"), n + 1)
                    step(v.tensor_tensor(coef, act_a, best.rearrange("p h k -> p (h k)"), ALU.mult))
                    if t + 1 < TILES:
                        wait_filled(v, "sc", l, TILES - 1, 3)
                        step(v.tensor_tensor(spread_w, bc(ident, [P, PE_PICKS, P], 1),
                                             bc(coef[:, 0:PE_PICKS], [P, PE_PICKS, P], 2), ALU.mult))
                        v.sem_inc(sem("weights_spread"), 1)
                        pick_experts(t + 1)
                        v.wait_ge(sem("v_summed"), l * (TILES - 1) + t + 1)
                        for hf in range(2):
                            empties(v, v.tensor_copy(acc[:, hf * 512:(hf + 1) * 512],
                                                     bank[turn["vsum", l, t, hf][0]]), "vsum", l, t, hf)
                    else:
                        step(v.memset(acc, 0.0))
                    first = PE_ROUNDS if t + 1 < TILES else 0
                    rounds = n * ROUNDS - (l * (TILES - 1) + t) * PE_ROUNDS
                    with v.Fori(first // 2, ROUNDS // 2) as k:
                        for half in range(2):
                            c8 = k * 2 + half
                            v.tensor_copy(coefs[:, half, :], coef[:, bass.ds(c8 * SLOTS, SLOTS)])\
                             .then_inc(sem("coefs_ready"), 1)
                            v.wait_ge(sem("coefs_ready"), c8 + (rounds - first + 1))
                            for j in range(SLOTS):
                                v.wait_ge(sem(f"row{j}_loaded"), (c8 + (2 * n * ROUNDS + ROUNDS + 1)) * 16)
                                v.scalar_tensor_tensor(out=acc, in0=rows[:, j, :], scalar=coefs[:, half, j:j + 1],
                                                       in1=acc, op0=ALU.mult, op1=ALU.add)\
                                 .then_inc(sem("rows_free"), 1)
                                v.wait_ge(sem("rows_free"), c8 * SLOTS + (used0 + PICKS + SLOTS + j + 1))
                    v.wait_ge(sem("gl2_loaded"), 16 * (4 * l + (3 if t == 0 else 4)))
                    step(v.tensor_tensor(acc, acc, gl2[:, 0, :], ALU.mult))
                    step(v.scalar_tensor_tensor(out=x[:, t, :], in0=x[:, t, :], scalar=ALPHA, in1=acc,
                                                op0=ALU.mult, op1=ALU.add))
                    layer_norm(x[:, t, :], gl2[:, 1, :], gl2[:, 2, :])
                    v.sem_inc(sem("x_final"), 1)

        @block.gpsimd
        def _(g):
            done = [0]

            def powers(count):
                for _ in range(count):
                    done[0] += 1
                    g.wait_ge(sem("squares_ready"), done[0])
                    g.tensor_tensor(rs, ms, nhalf, ALU.pow).then_inc(sem("roots_ready"), 1)

            g.memset(ms, 1.0).then_inc(sem("ms_set"), 1)
            g.wait_ge(sem("ms_set"), 1)
            g.wait_ge(sem("consts_loaded"), 16)
            for l in range(DEPTH):
                powers(2 * TILES)
                g.wait_ge(sem("ak_ready"), l + 1)
                wait_emptied(g, "proj", l, BLK["akv"], 0)
                kv = sem("kv_stored")
                g.dma_start(new_a_k[0, l].rearrange("t g d -> t (g d)"), akv[:, 0, 0:128]).then_inc(kv, 16)
                g.dma_start(new_a_v[0, l].rearrange("t g d -> t (g d)"), akv[:, 0, 128:256]).then_inc(kv, 16)
                wait_emptied(g, "proj", l, BLK["dk"], 0)
                wait_emptied(g, "proj", l, BLK["dv"], 0)
                g.dma_start(new_d_k[0, l].rearrange("t h j d -> t (h j d)"), dk[:, 0, :]).then_inc(kv, 16)
                g.dma_start(new_d_v[0, l].rearrange("t h d -> t (h d)"), dv[:, 0, :]).then_inc(kv, 16)
                powers(2 * TILES)
                g.wait_ge(sem("c_new_ready"), 2 * (l + 1))
                g.wait_ge(sem("m_out_ready"), l + 1)
                st = sem("state_stored")
                for a in range(2):
                    g.dma_start(new_c_C[0, l, a].rearrange("h d e -> d h e"), c_new[:, a, :, 0:CD]).then_inc(st, 16)
                with nc.allow_non_contiguous_dma("one column of the states"):
                    for a in range(2):
                        g.dma_start(new_c_n[0, l, a].rearrange("h d -> d h"), c_new[:, a, :, CD]).then_inc(st, 16)
                g.dma_start(new_c_m[0, l].rearrange("a h -> (a h)").unsqueeze(0),
                            m_out[0:1].rearrange("p a h -> p (a h)")).then_inc(st, 16)
                powers(TILES)
                powers(TILES)
                for t in range(TILES):
                    n = n_of(l, t)
                    g.wait_ge(sem("idx_ready"), n + 1)
                    if t == 0:
                        wait_filled(g, "q", l, Q_HEADS[4 * 3 - 1])
                    for phase, table in enumerate((peer_u, peer_v)):
                        flat = table.rearrange("l e d -> (l e) d")
                        base = (2 * n + phase) * ROUNDS

                        def gather(r, half):
                            g.wait_ge(sem("rows_free"), r * SLOTS + (base * SLOTS + 1))
                            g.sem_inc(sem("slots_claimed"), 1)
                            g.tensor_copy(idx_slot[:, half, :], idx[:, n % 2, bass.ds(r * SLOTS, SLOTS)])\
                             .then_inc(sem("indices_ready"), 1)
                            g.wait_ge(sem("indices_ready"), r + (base + 1))
                            g.sem_inc(sem("slots_claimed"), 1)
                            for j in range(SLOTS):
                                g.wait_ge(sem("rows_free"), r * SLOTS + (base * SLOTS + j + 1))
                                g.sem_inc(sem("slots_claimed"), 1)
                                g.indirect_dma_start(rows[:, j, :], None, flat,
                                                     bass.IndirectOffsetOnAxis(ap=idx_slot[:, half, j:j + 1], axis=0))\
                                 .then_inc(sem(f"row{j}_loaded"), 16)

                        gather(0, 0)
                        if t and phase == 0:
                            powers(1)
                        with g.Fori(0, ROUNDS // 2 - 1) as k:
                            gather(k * 2 + 1, 1)
                            gather(k * 2 + 2, 0)
                        gather(ROUNDS - 1, 1)
                powers(1)
            g.wait_ge(sem("kv_stored"), 64 * DEPTH)
            g.wait_ge(sem("state_stored"), 16 * 5 * DEPTH)


_INS = ["x_prompt", "x_sample", "cache_a_k", "cache_a_v", "cache_d_k", "cache_d_v", "state_c_C", "state_c_n",
        "state_c_m", "c", "c_ctx", "w_mod", "b_mod", "w_in", "attn_qk_gain", "gmlp_ws", "gmlp_b",
        "mlstm_gate_bias", "mlstm_gn", "diff_lambda", "diff_gn", "w_branch", "w_out", "ln_g", "ln_b",
        "peer_wq", "peer_keys", "peer_u", "peer_v"]
_OUTS = [(1, P, DM), (1, 2 * P, DM), (1, DEPTH, P, AG, AD), (1, DEPTH, P, AG, AD), (1, DEPTH, P, DH, 2, DD),
         (1, DEPTH, P, DH, DV), (1, DEPTH, 2, CH, CD, CD), (1, DEPTH, 2, CH, CD), (1, DEPTH, 2, CH)]


def constants(np):
    out = np.zeros((P, 1056), np.float32)
    s, t = np.arange(P)[:, None], np.arange(P)[None, :]
    out[:, 0:128] = s == t
    out[:, 128:256] = 1.0
    out[:, 256:384] = s <= t
    out[:, 384:512] = s >= t
    out[:, 512:640] = np.where(t <= s, 0.0, NEG)
    out[:, 640:768] = np.where(t >= s, 0.0, NEG)
    quarter = AD // 4
    inv = np.float32(10000.0) ** (-np.arange(quarter, dtype=np.float32) / np.float32(quarter))
    cos, sin = np.zeros((2 * P, 2, 2, quarter)), np.zeros((2 * P, 2, 2, quarter))
    token = np.arange(2 * P)
    for a, at in enumerate((token // GW, token % GW)):
        ang = (at[:, None].astype(np.float32) * inv[None, :]).astype(np.float32).astype(np.float64)
        cos[:, a, 0], cos[:, a, 1] = np.cos(ang), np.cos(ang)
        sin[:, a, 0], sin[:, a, 1] = -np.sin(ang), np.sin(ang)
    tables = np.stack([cos.reshape(2, P, AD), sin.reshape(2, P, AD)])
    out[:, 768:1024] = tables.transpose(2, 0, 1, 3).reshape(P, 256)
    out[:, 1024:1040] = np.arange(16)
    out[:, 1040:1056] = -0.5
    return out


def kernel(**inputs):
    import numpy as np
    import concourse.bacc as bacc
    from concourse.bass_utils import run_bass_kernel_spmd

    nc = bacc.Bacc("TRN2", target_bir_lowering=False, num_devices=1)
    arrays, args = {}, []
    for name in _INS:
        a = np.ascontiguousarray(inputs[name])
        arrays[f"in_{name}"] = a
        args.append(nc.dram_tensor(f"in_{name}", a.shape, mybir.dt.float32, kind="ExternalInput").ap())
    arrays["in_consts"] = constants(np)
    args.append(nc.dram_tensor("in_consts", (P, 1056), mybir.dt.float32, kind="ExternalInput").ap())
    for i, shape in enumerate(_OUTS):
        args.append(nc.dram_tensor(f"out_{i}", shape, mybir.dt.float32, kind="ExternalOutput").ap())
    build(nc, *args)
    r = run_bass_kernel_spmd(nc, [arrays], core_ids=[0])
    return tuple(np.asarray(r.results[0][f"out_{i}"]) for i in range(len(_OUTS)))
```
